# Optimizing a Trainium2 kernel written in Bass

```python
import math
import jax, jax.numpy as jnp
from jax import lax
import numpy as np

D_MODEL = 1024
BATCH = 1
SEQ = 256
DEPTH = 1

N_Q_HEADS = 8
N_KV_HEADS = 4
GQA_GROUP = N_Q_HEADS // N_KV_HEADS
HEAD_DIM = 128
WINDOW = 128
BLOCK = 128
N_HALO = -(-WINDOW // BLOCK)
NEG_INF = -1e30
CONV_CH = D_MODEL
CONV_WIDTH = 31
CONV_PAD = (CONV_WIDTH - 1) // 2
CONV_IN_W = 2 * CONV_CH
Q_W = N_Q_HEADS * HEAD_DIM
KV_W = N_KV_HEADS * HEAD_DIM
GATE_W = 2 * D_MODEL
Q_OFF = CONV_IN_W
K_OFF = Q_OFF + Q_W
V_OFF = K_OFF + KV_W
G_OFF = V_OFF + KV_W
IN_WIDTH = G_OFF + GATE_W
N_GROUPS = 4
EXPERTS_PER_GROUP = 8
N_EXPERTS = N_GROUPS * EXPERTS_PER_GROUP
TOP_K = 2
EXPERT_HIDDEN = D_MODEL // 4
LN_EPS = 1e-5
DEEPNORM_ALPHA = (2.0 * DEPTH) ** 0.25
DEEPNORM_BETA = (8.0 * DEPTH) ** -0.25

kernel_name = "hybrid_conv_swa_hmoe_encoder"

def layer_norm(x, g, b):
    xf = x.astype(jnp.float32)
    mu = xf.mean(-1, keepdims=True)
    var = jnp.square(xf - mu).mean(-1, keepdims=True)
    return ((xf - mu) * lax.rsqrt(var + LN_EPS) * g + b).astype(x.dtype)

def conformer_conv(u, w_dw, b_dw, ln_g, ln_b, w_proj):
    a, gate = jnp.split(u, 2, axis=-1)
    h = a * jax.nn.sigmoid(gate)
    h = lax.conv_general_dilated(
        h, w_dw[:, None, :].astype(h.dtype), window_strides=(1,),
        padding=((CONV_PAD, CONV_PAD),),
        dimension_numbers=("NWC", "WIO", "NWC"),
        feature_group_count=CONV_CH) + b_dw
    h = jax.nn.silu(layer_norm(h, ln_g, ln_b))
    return h @ w_proj

def windowed_gqa(q, k, v, sink, slopes):
    B, S = q.shape[0], q.shape[1]
    nb = S // BLOCK
    span = (2 * N_HALO + 1) * BLOCK
    qb = q.reshape(B, nb, BLOCK, N_KV_HEADS, GQA_GROUP, HEAD_DIM)

    def band(t):
        tp = jnp.pad(t, ((0, 0), (N_HALO * BLOCK, N_HALO * BLOCK), (0, 0), (0, 0)))
        tp = tp.reshape(B, nb + 2 * N_HALO, BLOCK, N_KV_HEADS, HEAD_DIM)
        return jnp.concatenate([tp[:, o:o + nb] for o in range(2 * N_HALO + 1)], axis=2)

    kb, vb = band(k), band(v)
    s = jnp.einsum("bnqhgd,bnshd->bnhgqs", qb, kb,
                   preferred_element_type=jnp.float32) * (HEAD_DIM ** -0.5)
    qi = jnp.arange(BLOCK)[:, None]
    kj = jnp.arange(span)[None, :]
    rel = kj - N_HALO * BLOCK - qi
    kpos = jnp.arange(nb)[:, None, None] * BLOCK - N_HALO * BLOCK + kj
    valid = (jnp.abs(rel) <= WINDOW)[None] & (kpos >= 0) & (kpos < S)
    dist = jnp.abs(rel).astype(jnp.float32)
    alibi = -slopes.reshape(N_KV_HEADS, GQA_GROUP)[:, :, None, None] * dist
    s = jnp.where(valid[None, :, None, None], s + alibi, NEG_INF)
    sk = sink.astype(jnp.float32).reshape(N_KV_HEADS, GQA_GROUP)[:, :, None, None]
    m = jnp.maximum(s.max(-1, keepdims=True), sk)
    p = jnp.exp(s - m)
    p = p / (p.sum(-1, keepdims=True) + jnp.exp(sk - m))
    o = jnp.einsum("bnhgqs,bnshd->bnqhgd", p.astype(v.dtype), vb)
    return o.reshape(B, S, Q_W).astype(q.dtype)

def hierarchical_moe(x, w_rg, b_rg, w_re, b_re, w_gate_up, w_down):
    B, S, D = x.shape
    t = x.reshape(B * S, D)
    g_logits = (t @ w_rg + b_rg).astype(jnp.float32)
    g_prob = jax.nn.softmax(g_logits, axis=-1)
    g_idx = jnp.argmax(g_logits, axis=-1)
    g_w = jnp.take_along_axis(g_prob, g_idx[:, None], axis=-1)
    e_logits = (t @ w_re + b_re).astype(jnp.float32).reshape(-1, N_GROUPS, EXPERTS_PER_GROUP)
    e_in = jnp.take_along_axis(e_logits, g_idx[:, None, None], axis=1)[:, 0]
    e_prob = jax.nn.softmax(e_in, axis=-1)
    top_w, top_i = lax.top_k(e_prob, TOP_K)
    top_w = top_w / top_w.sum(-1, keepdims=True)
    expert_id = g_idx[:, None] * EXPERTS_PER_GROUP + top_i
    weight = g_w * top_w
    comb = (jax.nn.one_hot(expert_id, N_EXPERTS, dtype=jnp.float32) * weight[..., None]).sum(1)
    out = jnp.zeros((B * S, D), jnp.float32)
    for e in range(N_EXPERTS):
        hg, hu = jnp.split(t @ w_gate_up[e], 2, axis=-1)
        out = out + comb[:, e:e + 1] * ((jax.nn.silu(hg) * hu) @ w_down[e])
    return out.astype(x.dtype).reshape(B, S, D)

def setup_inputs(seed: int = 0) -> dict:
    key = jax.random.key(seed)
    ks = jax.random.split(key, 24)
    L, D = DEPTH, D_MODEL
    f32 = jnp.float32

    def nrm(k, shape, scale):
        return jax.random.normal(k, shape, f32) * scale

    x = nrm(ks[0], (BATCH, SEQ, D), 1.0)
    w_in = nrm(ks[1], (L, D, IN_WIDTH), D ** -0.5)
    w_in = w_in.at[:, :, V_OFF:V_OFF + KV_W].multiply(DEEPNORM_BETA)
    return {
        "x": x,
        "w_in": w_in,
        "b_gate": nrm(ks[2], (L, GATE_W), 0.02),
        "w_dw": nrm(ks[3], (L, CONV_WIDTH, CONV_CH), CONV_WIDTH ** -0.5),
        "b_dw": nrm(ks[4], (L, CONV_CH), 0.02),
        "conv_ln_g": 1.0 + nrm(ks[5], (L, CONV_CH), 0.02),
        "conv_ln_b": nrm(ks[6], (L, CONV_CH), 0.02),
        "w_conv_proj": nrm(ks[7], (L, CONV_CH, D), CONV_CH ** -0.5),
        "attn_sink": nrm(ks[8], (L, N_Q_HEADS), 0.5),
        "w_attn_proj": nrm(ks[9], (L, Q_W, D), Q_W ** -0.5),
        "w_out": nrm(ks[10], (L, D, D), D ** -0.5 * DEEPNORM_BETA),
        "ln1_g": 1.0 + nrm(ks[11], (L, D), 0.02),
        "ln1_b": nrm(ks[12], (L, D), 0.02),
        "w_router_group": nrm(ks[13], (L, D, N_GROUPS), D ** -0.5),
        "b_router_group": nrm(ks[14], (L, N_GROUPS), 0.01),
        "w_router_expert": nrm(ks[15], (L, D, N_EXPERTS), D ** -0.5),
        "b_router_expert": nrm(ks[16], (L, N_EXPERTS), 0.01),
        "w_gate_up": nrm(ks[17], (L, N_EXPERTS, D, 2 * EXPERT_HIDDEN), D ** -0.5),
        "w_down": nrm(ks[18], (L, N_EXPERTS, EXPERT_HIDDEN, D), EXPERT_HIDDEN ** -0.5 * DEEPNORM_BETA),
        "ln2_g": 1.0 + nrm(ks[19], (L, D), 0.02),
        "ln2_b": nrm(ks[20], (L, D), 0.02),
    }

def reference(x, w_in, b_gate, w_dw, b_dw, conv_ln_g, conv_ln_b, w_conv_proj, attn_sink,
              w_attn_proj, w_out, ln1_g, ln1_b, w_router_group, b_router_group,
              w_router_expert, b_router_expert, w_gate_up, w_down, ln2_g, ln2_b):
    B, S, _ = x.shape
    slopes = jnp.exp2(-8.0 * jnp.arange(1, N_Q_HEADS + 1, dtype=jnp.float32) / N_Q_HEADS)
    for l in range(DEPTH):
        proj = x @ w_in[l]
        conv_u = proj[..., :Q_OFF]
        q = proj[..., Q_OFF:K_OFF].reshape(B, S, N_Q_HEADS, HEAD_DIM)
        k = proj[..., K_OFF:V_OFF].reshape(B, S, N_KV_HEADS, HEAD_DIM)
        v = proj[..., V_OFF:G_OFF].reshape(B, S, N_KV_HEADS, HEAD_DIM)
        gates = jax.nn.sigmoid(proj[..., G_OFF:] + b_gate[l])
        g_conv, g_attn = gates[..., :D_MODEL], gates[..., D_MODEL:]
        conv_out = conformer_conv(conv_u, w_dw[l], b_dw[l], conv_ln_g[l], conv_ln_b[l], w_conv_proj[l])
        attn_out = windowed_gqa(q, k, v, attn_sink[l], slopes) @ w_attn_proj[l]
        mixed = (g_conv * conv_out + g_attn * attn_out) @ w_out[l]
        x = layer_norm(DEEPNORM_ALPHA * x + mixed, ln1_g[l], ln1_b[l])
        moe = hierarchical_moe(x, w_router_group[l], b_router_group[l], w_router_expert[l],
                               b_router_expert[l], w_gate_up[l], w_down[l])
        x = layer_norm(DEEPNORM_ALPHA * x + moe, ln2_g[l], ln2_b[l])
    return x


_drawn_inputs = setup_inputs


def setup_inputs(seed=0):
    import zlib

    import numpy as np

    out = dict(_drawn_inputs(seed))
    spreads = {}
    factors = {'b_gate': 8.0,
     'b_dw': 7.782,
     'conv_ln_g': 8.0,
     'conv_ln_b': 8.0,
     'attn_sink': 42.046,
     'b_router_group': 5.963,
     'b_router_expert': 17.347,
     'ln2_g': 8.122,
     'ln2_b': 8.38}
    for name, (base, spread) in spreads.items():
        noise = np.random.default_rng([zlib.crc32(name.encode()), seed]).standard_normal(out[name].shape)
        drawn = base * np.exp(spread * noise) if base else spread * noise
        out[name] = __import__('jax').numpy.asarray(drawn.astype(out[name].dtype))
    for name, factor in factors.items():
        out[name] = (out[name] * factor).astype(out[name].dtype)
    return out
```

```python
from contextlib import ExitStack

import concourse.bass as bass
import numpy as np
from concourse import mybir

F32 = mybir.dt.float32
F32R = mybir.dt.float32r
I32 = mybir.dt.int32
ALU = mybir.AluOpType
ACT = mybir.ActivationFunctionType
X_AXIS = mybir.AxisListType.X

P = 128
D = 1024
SEQ = 256
HEADS, KV_HEADS = 8, 4
CONV_WIDTH = 31
PAD = (CONV_WIDTH - 1) // 2
WINDOW = 128
GROUPS, PER_GROUP = 4, 8
EXPERTS = GROUPS * PER_GROUP
HIDDEN = D // 4
LN_EPS = 1e-5
ALPHA = 2.0 ** 0.25
SCALE = float(P) ** -0.5
FAR = 3e32
NEVER = 1e30

KT = D // P
TT = SEQ // P
HT = HIDDEN // P
LOGITS = GROUPS + EXPERTS
HALF = 512

ORDER = [c for i in range(KT) for c in (i, KT + i)]
ORDER += list(range(16, 32)) + list(range(40, 48)) + list(range(32, 40))
N_IN = len(ORDER)
B_ATTN, B_CONV, B_OUT = N_IN, N_IN + KT, N_IN + 2 * KT
N_BLOCKS = N_IN + 3 * KT
Q_BLOCK, V_BLOCK, GATE_BLOCK = 16, 28, 32
N_PAIRS = B_OUT // 2

RAW = 3
SPLIT = 2
PSUM_PAIRS = 3
TAPS_PER_BLOCK = 5

WIN = 64
PAIRS = EXPERTS // 2
SLOTS = 4
GU_N = KT * 2 * HIDDEN
WD_N = HT * D
SLOT_N = GU_N + WD_N

C_IDENT, C_DIST, C_TRI, C_SEL, C_IOTA = 0, 128, 128 + 512, 768, 832
C_RANK4 = C_IOTA + WIN
C_RANK32 = C_RANK4 + GROUPS
C_END = C_RANK32 + EXPERTS
A_BGATE = 0
A_WDW = 16
A_BDW = A_WDW + KT * CONV_WIDTH
A_LNG = A_BDW + KT
A_LNB = A_LNG + KT
A_END = A_LNB + KT
R_BIAS, R_SINK, R_END = 0, LOGITS, LOGITS + HEADS


def constants():
    c = np.zeros((P, C_END), np.float32)
    c[:, C_IDENT:C_IDENT + P] = np.eye(P)
    q = np.arange(P)[:, None, None] + P * np.arange(TT)[None, :, None]
    dist = np.abs(q - np.arange(SEQ)[None, None, :]).astype(np.float32)
    c[:, C_DIST:C_DIST + TT * SEQ] = np.where(dist <= WINDOW, dist, FAR).reshape(P, TT * SEQ)
    c[:, C_TRI:C_TRI + P] = np.arange(P)[:, None] < np.arange(P)[None, :]
    c[:, C_SEL:C_SEL + WIN] = np.arange(P)[:, None] % WIN == np.arange(WIN)[None, :]
    c[:, C_IOTA:C_IOTA + WIN] = np.arange(1, WIN + 1)
    c[:, C_RANK4:C_RANK4 + GROUPS] = np.arange(GROUPS, 0, -1)
    c[:, C_RANK32:C_RANK32 + EXPERTS] = np.arange(EXPERTS, 0, -1)
    return c


def encoder_kernel(nc, xT, x, consts, chan, rows, w_in, w_attn, w_conv, w_out, ln1, ln2, w_router,
                   w_gate_up, w_down, out):
    with ExitStack() as ctx:
        def sb(name, shape, dt=F32):
            return ctx.enter_context(nc.sbuf_tensor(name, shape, dt))

        def sem(name):
            return ctx.enter_context(nc.semaphore(name))

        slots = sb("slots", [P, SLOTS, SLOT_N])
        con = sb("con", [P, C_END])
        par = sb("par", [P, A_END])
        row = sb("row", [P, R_END])
        xt = sb("xt", [P, TT, D])
        raw = sb("raw", [P, RAW, D])
        gates = sb("gates", [P, 16, SEQ])
        kT = sb("kT", [P, KV_HEADS, SEQ])
        vT = sb("vT", [P, KV_HEADS, SEQ])
        pT = sb("pT", [P, 2, TT, SEQ])
        sig = sb("sig", [P, 2, SEQ])
        wr = sb("wr", [P, KT, LOGITS])
        x_hi, x_lo = sb("x_hi", [P, KT, SEQ], F32R), sb("x_lo", [P, KT, SEQ], F32R)
        a_hi, a_lo = sb("a_hi", [P, KT, SEQ], F32R), sb("a_lo", [P, KT, SEQ], F32R)
        w_hi, w_lo = sb("w_hi", [P, SPLIT, D], F32R), sb("w_lo", [P, SPLIT, D], F32R)
        ones = sb("ones", [P, P])
        mean_ones = sb("mean_ones", [P, P])
        eps = sb("eps", [P, 1])
        small = sb("small", [P, 8, 2 * HEADS])
        stat = sb("stat", [P, TT, 2, 6])
        mv = sb("mv", [P, TT, 4])
        rt = sb("rt", [P, 8, TT, EXPERTS])
        rs = sb("rs", [P, 16, TT])
        rg = sb("rg", [P, 4, TT, GROUPS])
        lg = sb("lg", [P, TT, LOGITS])
        load_f = sb("load_f", [1, 1])
        load_i = sb("load_i", [1, 1], I32)

        over = slots[:, 2:4, :].rearrange("p s n -> p (s n)")
        at = [0]

        def carve(n):
            at[0] += n
            return over[:, at[0] - n:at[0]]

        h_pad = carve(KT * (SEQ + 2 * PAD)).rearrange("p (i t) -> p i t", i=KT)
        acc = carve(KT * SEQ).rearrange("p (i t) -> p i t", i=KT)
        qT = carve(HEADS * SEQ).rearrange("p (i t) -> p i t", i=HEADS)
        v_sb = carve(TT * KV_HEADS * P).rearrange("p (t n) -> p t n", t=TT)
        prob = carve(HEADS * TT * SEQ).rearrange("p (h t n) -> p h t n", h=HEADS, t=TT)
        assert at[0] <= 2 * SLOT_N
        square = h_pad.rearrange("p i t -> p (i t)")[:, 0:KT * SEQ].rearrange("p (i t) -> p i t", i=KT)
        xT_raw = gates[:, 0:KT, :]
        ln_rows = gates[:, 0:8, :].rearrange("p (a b) t -> p a (b t)", a=2)
        ln2_rows = gates[:, 8:16, :].rearrange("p (a b) t -> p a (b t)", a=2)
        x1T = raw[:, 0:2, :].rearrange("p a (b t) -> p (a b) t", t=SEQ)

        x1_hi = x_hi[:].rearrange("p i t -> p (i t)").rearrange("p (t n) -> p t n", t=TT)
        x1_lo = x_lo[:].rearrange("p i t -> p (i t)").rearrange("p (t n) -> p t n", t=TT)
        y_hi = w_hi[:, 0, :]
        y_lo = w_lo[:, 0, :]
        gat = [w_hi[:, 1, 256 * i:256 * i + 256].rearrange("p (t n) -> p t n", t=TT) for i in range(2)]
        sca = [w_lo[:, 1, 256 * i:256 * i + 256] for i in range(2)]
        xg = [raw[:, i, :].rearrange("p (k n) -> p k n", k=KT) for i in range(2)]
        gu = [pT[:, i, :, :].rearrange("p a t -> p (a t)") for i in range(2)]
        hT = vT[:, 0:1, :].rearrange("p a (j k n) -> p (a j) k n", j=2, k=HT)
        silu = vT[:, 1:2, :].rearrange("p a (j k n) -> p (a j) k n", j=2, k=HT)
        weight = [vT[:, 2, i:i + 1] for i in range(2)]
        comb = [vT[:, 2, 16 * i + 16:16 * i + 20].rearrange("p (t j) -> p t j", t=TT) for i in range(2)]
        more_place = vT[:, 2, 48:52].rearrange("p (t j) -> p t j", t=TT)

        ident = con[:, C_IDENT:C_IDENT + P]
        dist = con[:, C_DIST:C_DIST + TT * SEQ]
        tri = con[:, C_TRI:C_TRI + P]
        sel = con[:, C_SEL:C_SEL + WIN]
        iota = con[:, C_IOTA:C_IOTA + WIN]
        rank4 = con[:, C_RANK4:C_RANK4 + GROUPS]
        rank32 = con[:, C_RANK32:C_RANK32 + EXPERTS]

        bank = [ctx.enter_context(nc.psum_tensor(f"bank{i}", [P, HALF], F32)) for i in range(8)]
        pair_bank = bank[0:3]
        score_bank = bank[3:5]
        t_bank, o_bank = bank[5], [bank[6], bank[7]]
        out_bank = [bank[3], bank[4], bank[5], bank[6]]
        moe_bank = out_bank
        gu_bank = [bank[0], bank[1]]
        y_bank = gu_bank
        h_bank, g_bank = bank[2], bank[7]

        s_xT, s_con, s_par, s_row, s_xt = (sem(n) for n in ("s_xT", "s_con", "s_par", "s_row", "s_xt"))
        s_ln1, s_ln2, s_wr, s_out = (sem(n) for n in ("s_ln1", "s_ln2", "s_wr", "s_out"))
        raw_loaded = [sem(f"raw_loaded{i}") for i in range(RAW)]
        gu_loaded = [sem(f"gu_loaded{i}") for i in range(SLOTS)]
        wd_loaded = [sem(f"wd_loaded{i}") for i in range(SLOTS)]
        consts_set = sem("consts_set")
        x_hi_done, x_lo_done = sem("x_hi_done"), sem("x_lo_done")
        w_hi_done, w_lo_done = sem("w_hi_done"), sem("w_lo_done")
        block_done = sem("block_done")
        sigmoid_done, glu_done = sem("sigmoid_done"), sem("glu_done")
        qkv_copied, gates_done = sem("qkv_copied"), sem("gates_done")
        taps_done = sem("taps_done")
        scores_done, scores_read, row_max_done = sem("scores_done"), sem("scores_read"), sem("row_max_done")
        neg_max_done, exp_done, sink_in, sink_exp = (sem(n) for n in ("neg_max_done", "exp_done", "sink_in", "sink_exp"))
        v_turned, v_copied = sem("v_turned"), sem("v_copied")
        prob_ready, p_turned, p_copied = sem("prob_ready"), sem("p_turned"), sem("p_copied")
        pv_done, o_hi_done, o_lo_done = sem("pv_done"), sem("o_hi_done"), sem("o_lo_done")
        attn_gated, conv_gated, merged = sem("attn_gated"), sem("conv_gated"), sem("merged")
        m_hi_done, m_lo_done = sem("m_hi_done"), sem("m_lo_done")
        mean_done, centered, squared, var_done = (sem(n) for n in ("mean_done", "centered", "squared", "var_done"))
        std_done, scaled, silu_done, c_hi_done, c_lo_done = (
            sem(n) for n in ("std_done", "scaled", "silu_done", "c_hi_done", "c_lo_done"))
        dve_step = sem("dve_step")
        ln_var, ln_std, x1_ready, x1_hi_done, x1_lo_done = (
            sem(n) for n in ("ln_var", "ln_std", "x1_ready", "x1_hi_done", "x1_lo_done"))
        x1_turned, x1T_copied, logits_done = sem("x1_turned"), sem("x1T_copied"), sem("logits_done")
        exp_in, router_exp, onehot_done, ranks_done, route_done, load_known = (
            sem(n) for n in ("exp_in", "router_exp", "onehot_done", "ranks_done", "route_done", "load_known"))
        gat_built, gathered, xg_copied = sem("gat_built"), sem("gathered"), sem("xg_copied")
        sca_turned, sca_copied = sem("sca_turned"), sem("sca_copied")
        gu_done, gu_copied0, gu_copied1 = sem("gu_done"), sem("gu_copied0"), sem("gu_copied1")
        h_summed, moe_silu, h_ready = sem("h_summed"), sem("moe_silu"), sem("h_ready")
        down_done, y_hi_done, y_lo_done, scattered = (
            sem(n) for n in ("down_done", "y_hi_done", "y_lo_done", "scattered"))
        more_loaded, more_copied = sem("more_loaded"), sem("more_copied")
        result = sem("result")

        def from_pair(p, n):
            return not isinstance(p, int) or p >= n

        def block_of(b):
            if b < B_ATTN:
                return w_in[ORDER[b]]
            if b < B_CONV:
                return w_attn[b - B_ATTN]
            if b < B_OUT:
                return w_conv[b - B_CONV]
            return w_out[(b - B_OUT) * P:(b - B_OUT + 1) * P, :]

        def wait_pair_read(eng, q):
            if q < Q_BLOCK // 2:
                eng.wait_ge(glu_done, q + 1)
            elif q < GATE_BLOCK // 2:
                eng.wait_ge(qkv_copied, q - Q_BLOCK // 2 + 1)
            elif q < N_IN // 2:
                eng.wait_ge(gates_done, q - GATE_BLOCK // 2 + 1)
            elif q < B_CONV // 2:
                eng.wait_ge(attn_gated, q - N_IN // 2 + 1)
            else:
                eng.wait_ge(conv_gated, q - B_CONV // 2 + 1)

        def last_head_step(h):
            return 38 + h

        block = ctx.enter_context(nc.Block())

        @block.sync
        def _(sp):
            def load_gate_up(e):
                sp.dma_start(slots[:, e % SLOTS, 0:GU_N], w_gate_up[e]).then_inc(gu_loaded[e % SLOTS], 16)

            def load_down(e):
                sp.dma_start(slots[:, e % SLOTS, GU_N:SLOT_N], w_down[e]).then_inc(wd_loaded[e % SLOTS], 16)

            sp.dma_start(xT_raw, xT).then_inc(s_xT, 16)
            for b in range(N_BLOCKS):
                if b >= RAW:
                    sp.wait_ge(w_lo_done, b - RAW + 1)
                sp.dma_start(raw[:, b % RAW, :], block_of(b)).then_inc(raw_loaded[b % RAW], 16)
                if b == 2:
                    sp.dma_start(par[:], chan).then_inc(s_par, 16)
                    sp.dma_start(con[:], consts).then_inc(s_con, 16)
                    sp.dma_start(row[:], rows.broadcast_to([P, R_END])).then_inc(s_row, 16)
                if b == 10:
                    load_gate_up(0)
                if b == 14:
                    load_gate_up(1)
                if b == 18:
                    load_down(0)
                    load_down(1)
                if b == 22:
                    sp.dma_start(xt[:], x.rearrange("(t p) n -> p t n", p=P)).then_inc(s_xt, 16)
                    sp.dma_start(wr[:], w_router).then_inc(s_wr, 16)
                if b == B_OUT + RAW:
                    sp.wait_ge(silu_done, KT)
                    sp.wait_ge(pv_done, HEADS)
                    load_gate_up(2)
                if b == B_OUT + RAW + 2:
                    load_gate_up(3)
            load_down(2)
            load_down(3)
            sp.wait_ge(m_lo_done, KT // 2)
            sp.dma_start(ln_rows, ln1.broadcast_to([P, 2, D])).then_inc(s_ln1, 16)
            sp.dma_start(ln2_rows, ln2.broadcast_to([P, 2, D])).then_inc(s_ln2, 16)
            sp.wait_ge(load_known, 1)
            load = sp.value_load(load_i[0:1, 0:1], min_val=0, max_val=SEQ)
            with sp.Fori(1, EXPERTS // SLOTS) as i:
                for s in range(SLOTS):
                    e = i * SLOTS + s
                    sp.wait_ge(gu_done, i * SLOTS + (s + 1 - SLOTS))
                    sp.dma_start(slots[:, s, 0:GU_N], w_gate_up[e]).then_inc(gu_loaded[s], 16)
                    sp.wait_ge(down_done, i * SLOTS + (s // 2 * 2 + 2 - SLOTS))
                    sp.dma_start(slots[:, s, GU_N:SLOT_N], w_down[e]).then_inc(wd_loaded[s], 16)
            with sp.If(load > WIN):
                with sp.Fori(0, EXPERTS) as e:
                    sp.wait_ge(scattered, e * 2 + PAIRS)
                    sp.dma_start(slots[:, 0, 0:GU_N], w_gate_up[e]).then_inc(more_loaded, 16)
                    sp.dma_start(slots[:, 0, GU_N:SLOT_N], w_down[e]).then_inc(more_loaded, 16)
            for t in range(TT):
                sp.wait_ge(result, t + 1)
                sp.dma_start(out[t * P:(t + 1) * P, :], xt[:, t, :]).then_inc(s_out, 16)
            sp.wait_ge(s_out, 16 * TT)

        @block.gpsimd
        def _(pool):
            nc.gpsimd.memset(h_pad, 0.0).then_inc(consts_set, 1)
            nc.gpsimd.memset(ones[:], 1.0).then_inc(consts_set, 1)
            nc.gpsimd.memset(mean_ones[:], 1.0 / D).then_inc(consts_set, 1)
            nc.gpsimd.memset(eps[:], LN_EPS).then_inc(consts_set, 1)

        @block.scalar
        def _(act):
            def split_hi(b):
                act.wait_ge(raw_loaded[b % RAW], 16 * (b // RAW + 1))
                if b >= SPLIT:
                    act.wait_ge(block_done, b - SPLIT + 1)
                nc.scalar.copy(w_hi[:, b % SPLIT, :], raw[:, b % RAW, :]).then_inc(w_hi_done, 1)

            def evacuate(q):
                src = pair_bank[q % PSUM_PAIRS]
                act.wait_ge(block_done, 2 * q + 2)
                if q < Q_BLOCK // 2:
                    if q >= 2:
                        act.wait_ge(glu_done, q - 1)
                    nc.scalar.activation(sig[:, q % 2, :], src[:, SEQ:], ACT.Sigmoid).then_inc(sigmoid_done, 1)
                elif q < GATE_BLOCK // 2:
                    n = 2 * (q - Q_BLOCK // 2)
                    dst = qT[:, n:n + 2, :] if n < HEADS else (
                        kT[:, n - 8:n - 6, :] if n < 12 else vT[:, n - 12:n - 10, :])
                    nc.scalar.copy(dst, src[:].rearrange("p (a t) -> p a t", a=2)).then_inc(qkv_copied, 1)
                elif q < N_IN // 2:
                    if q == GATE_BLOCK // 2:
                        act.wait_ge(s_par, 16)
                        act.wait_ge(x_lo_done, 1)
                    for j in range(2):
                        c = ORDER[2 * q + j] - GATE_BLOCK
                        ins = nc.scalar.activation(gates[:, c, :], src[:, j * SEQ:(j + 1) * SEQ], ACT.Sigmoid,
                                                   bias=par[:, A_BGATE + c:A_BGATE + c + 1])
                    ins.then_inc(gates_done, 1)
                elif q >= B_CONV // 2:
                    m = q - B_CONV // 2
                    act.wait_ge(merged, m + 1)
                    nc.scalar.copy(a_hi[:, 2 * m:2 * m + 2, :], gates[:, 2 * m:2 * m + 2, :]).then_inc(m_hi_done, 1)

            def exponentials(h):
                act.wait_ge(neg_max_done, h // 2 + 1)
                for t in range(TT):
                    ins = nc.scalar.activation(prob[:, h, t, :], prob[:, h, t, :], ACT.Exp, scale=SCALE,
                                               bias=small[:, 1, TT * h + t:TT * h + t + 1],
                                               accum_out=small[:, 2, TT * h + t:TT * h + t + 1])
                ins.then_inc(exp_done, 1)

            def copy_pT(h):
                act.wait_ge(p_turned, h + 1)
                if h >= 2:
                    act.wait_ge(pv_done, h - 1)
                nc.scalar.copy(pT[:, h % 2, :, :], t_bank[:].rearrange("p (a t) -> p a t", a=2)).then_inc(p_copied, 1)

            def split_o(h):
                act.wait_ge(pv_done, h + 1)
                nc.scalar.copy(a_hi[:, h, :], o_bank[h % 2][:, 0:SEQ]).then_inc(o_hi_done, 1)

            act.wait_ge(s_xT, 16)
            nc.scalar.copy(x_hi[:], xT_raw).then_inc(x_hi_done, 1)
            for b in range(N_BLOCKS):
                if b == B_CONV + SPLIT:
                    act.wait_ge(centered, 1)
                    nc.scalar.activation(square, acc, ACT.Square).then_inc(squared, 1)
                    act.wait_ge(var_done, 1)
                    act.wait_ge(consts_set, 4)
                    nc.scalar.activation(sig[:, 0, :], bank[7][:, SEQ:], ACT.Sqrt, bias=eps[:, 0:1]).then_inc(std_done, 1)
                    act.wait_ge(x_lo_done, 1)
                    for i in range(KT):
                        act.wait_ge(scaled, i + 1)
                        nc.scalar.activation(acc[:, i, :], acc[:, i, :], ACT.Silu,
                                             scale=par[:, A_LNG + i:A_LNG + i + 1],
                                             bias=par[:, A_LNB + i:A_LNB + i + 1]).then_inc(silu_done, 1)
                        act.wait_ge(silu_done, i + 1)
                        if i == 0:
                            act.wait_ge(block_done, N_IN)
                        nc.scalar.copy(x_hi[:, i, :], acc[:, i, :]).then_inc(c_hi_done, 1)
                split_hi(b)
                if b % 2 and b >= 3:
                    q = (b - 3) // 2
                    if q < N_PAIRS:
                        evacuate(q)
                if 31 <= b <= 34:
                    for h in (2 * (b - 31), 2 * (b - 31) + 1):
                        exponentials(h)
                    if b == 34:
                        act.wait_ge(sink_in, 1)
                        nc.scalar.activation(small[:, 4, :], small[:, 3, :], ACT.Exp).then_inc(sink_exp, 1)
                if 38 <= b < 38 + HEADS:
                    copy_pT(b - 38)
                if 39 <= b < 39 + HEADS:
                    split_o(b - 39)

            for t in range(TT):
                act.wait_ge(ln_var, t + 1)
                nc.scalar.activation(mv[:, t, 2:3], mv[:, t, 1:2], ACT.Sqrt, bias=eps[:, 0:1]).then_inc(ln_std, 1)
            for t in range(TT):
                act.wait_ge(x1_ready, t + 1)
                nc.scalar.copy(x1_hi[:, t, :], xt[:, t, :]).then_inc(x1_hi_done, 1)
                for c in range(2):
                    act.wait_ge(x1_turned, 2 * t + c + 1)
                    src = (pair_bank + [bank[7]])[2 * t + c]
                    nc.scalar.copy(x1T[:, 4 * c:4 * c + 4, t * P:(t + 1) * P],
                                   src[:].rearrange("p (a t) -> p a t", a=4)).then_inc(x1T_copied, 1)
            act.wait_ge(exp_in, 1)
            nc.scalar.activation(rg[:, 2, :, :], rg[:, 1, :, :], ACT.Exp).then_inc(router_exp, 1)
            act.wait_ge(exp_in, 2)
            nc.scalar.activation(rs[:, 8, :], rs[:, 7, :], ACT.Exp).then_inc(router_exp, 1)

            def take_gathered(p, u, c):
                act.wait_ge(gathered, 2 * p + (c + 1))
                if c == 0 and from_pair(p, 2):
                    act.wait_ge(gu_done, 2 * p - 2)
                nc.scalar.copy(xg[u][:, 4 * c:4 * c + 4, :],
                               g_bank[:].rearrange("p (k n) -> p k n", k=4)).then_inc(xg_copied, 1)

            def take_scatter(p, u):
                act.wait_ge(sca_turned, p + 1)
                if from_pair(p, 2):
                    act.wait_ge(scattered, p - 1)
                    act.wait_ge(y_lo_done, 2 * p - 2)
                nc.scalar.copy(sca[u], g_bank[:, 0:SEQ])
                for j in range(2):
                    ins = nc.scalar.copy(weight[u][j * WIN:(j + 1) * WIN, :],
                                         g_bank[j * WIN:(j + 1) * WIN, SEQ + j:SEQ + j + 1])
                ins.then_inc(sca_copied, 1)

            def take_gate_up(p):
                act.wait_ge(gu_done, 2 * p + 1)
                if from_pair(p, 1):
                    act.wait_ge(h_summed, p)
                nc.scalar.copy(gu[0], gu_bank[0][:]).then_inc(gu_copied0, 1)

            def swish(p):
                act.wait_ge(h_summed, p + 1)
                if from_pair(p, 1):
                    act.wait_ge(h_ready, p)
                nc.scalar.activation(silu, h_bank[:].rearrange("p (j c n) -> p j c n", j=2, c=4)[:, :, 0:HT, :],
                                     ACT.Silu).then_inc(moe_silu, 1)

            def weigh_hi(p, u):
                for c in range(2):
                    act.wait_ge(down_done, 2 * p + (c + 1))
                    if c == 0 and from_pair(p, 1):
                        act.wait_ge(scattered, p)
                    act.wait_ge(sca_copied, p + 1)
                    nc.scalar.activation(y_hi[:, c * HALF:(c + 1) * HALF], y_bank[c][:], ACT.Copy,
                                         scale=weight[u]).then_inc(y_hi_done, 1)

            def pair(p, u, last=False):
                take_gate_up(p)
                if not last:
                    take_gathered(p + 1, 1 - u, 0)
                    take_gathered(p + 1, 1 - u, 1)
                swish(p)
                if not last:
                    take_scatter(p + 1, 1 - u)
                weigh_hi(p, u)

            take_gathered(0, 0, 0)
            take_gathered(0, 0, 1)
            take_scatter(0, 0)
            for p in range(2):
                pair(p, p)
            with act.Fori(1, PAIRS // 2 - 1) as i:
                for u in range(2):
                    pair(i * 2 + u, u)
            for p in range(PAIRS - 2, PAIRS):
                pair(p, p % 2, last=(p == PAIRS - 1))
            load = act.value_load(load_i[0:1, 0:1], min_val=0, max_val=SEQ)
            with act.If(load > WIN):
                with act.Fori(0, EXPERTS) as e:
                    for u in range(2):
                        n = e * 2 + (PAIRS + u)
                        take_gathered(n, u, 0)
                        take_gathered(n, u, 1)
                        take_scatter(n, u)
                        take_gate_up(n)
                        swish(n)
                        weigh_hi(n, u)
            for t in range(TT):
                act.wait_ge(ln_var, TT + t + 1)
                nc.scalar.activation(mv[:, t, 2:3], mv[:, t, 1:2], ACT.Sqrt, bias=eps[:, 0:1]).then_inc(ln_std, 1)

        @block.vector
        def _(dve):
            steps = [0]

            def chained(ins):
                steps[0] += 1
                ins.then_inc(dve_step, 1)
                dve.wait_ge(dve_step, steps[0])

            def split_lo(b):
                dve.wait_ge(w_hi_done, b + 1)
                nc.vector.tensor_tensor(w_lo[:, b % SPLIT, :], raw[:, b % RAW, :],
                                        w_hi[:, b % SPLIT, :].bitcast(F32), ALU.subtract).then_inc(w_lo_done, 1)

            def conv_taps():
                n = 0
                for m in range(0, KT, 2):
                    for tap in range(CONV_WIDTH):
                        for i in (m, m + 1):
                            w = par[:, A_WDW + i * CONV_WIDTH + tap:A_WDW + i * CONV_WIDTH + tap + 1]
                            h = h_pad[:, i, tap:tap + SEQ]
                            if tap:
                                dve.wait_ge(taps_done, n - 1)
                                ins = nc.vector.scalar_tensor_tensor(acc[:, i, :], h, w, acc[:, i, :], ALU.mult, ALU.add)
                            else:
                                ins = nc.vector.tensor_scalar(acc[:, i, :], h, w, par[:, A_BDW + i:A_BDW + i + 1],
                                                              ALU.mult, ALU.add)
                            ins.then_inc(taps_done, 1)
                            n += 1
                            yield m

            taps = conv_taps()
            done = [0]

            def some_taps(count, ready):
                for _ in range(count):
                    m = done[0] // (2 * CONV_WIDTH) * 2
                    if m + 2 > ready or done[0] >= KT * CONV_WIDTH:
                        return
                    next(taps)
                    done[0] += 1

            def evacuate(q):
                src = pair_bank[q % PSUM_PAIRS]
                if q < Q_BLOCK // 2:
                    dve.wait_ge(sigmoid_done, q + 1)
                    nc.vector.tensor_tensor(h_pad[:, q, PAD:PAD + SEQ], src[:, 0:SEQ], sig[:, q % 2, :],
                                            ALU.mult).then_inc(glu_done, 1)
                    dve.wait_ge(glu_done, q + 1)
                elif N_IN // 2 <= q < B_CONV // 2:
                    m = q - N_IN // 2
                    dve.wait_ge(block_done, 2 * q + 2)
                    dve.wait_ge(gates_done, N_IN // 2 - GATE_BLOCK // 2)
                    g = gates[:, KT + 2 * m:KT + 2 * m + 2, :]
                    nc.vector.tensor_tensor(g, src[:].rearrange("p (a t) -> p a t", a=2), g,
                                            ALU.mult).then_inc(attn_gated, 1)
                elif q >= B_CONV // 2:
                    m = q - B_CONV // 2
                    g, other = gates[:, 2 * m:2 * m + 2, :], gates[:, KT + 2 * m:KT + 2 * m + 2, :]
                    dve.wait_ge(block_done, 2 * q + 2)
                    nc.vector.tensor_tensor(g, src[:].rearrange("p (a t) -> p a t", a=2), g,
                                            ALU.mult).then_inc(conv_gated, 1)
                    dve.wait_ge(conv_gated, m + 1)
                    dve.wait_ge(attn_gated, m + 1)
                    nc.vector.tensor_tensor(g, g, other, ALU.add).then_inc(merged, 1)
                    dve.wait_ge(m_hi_done, m + 1)
                    nc.vector.tensor_tensor(a_lo[:, 2 * m:2 * m + 2, :], g,
                                            a_hi[:, 2 * m:2 * m + 2, :].bitcast(F32),
                                            ALU.subtract).then_inc(m_lo_done, 1)

            def take_scores(h):
                dve.wait_ge(scores_done, h + 1)
                slope = 2.0 ** (-8.0 * (h + 1) / HEADS)
                nc.vector.scalar_tensor_tensor(prob[:, h, :, :].rearrange("p t n -> p (t n)"), dist, -slope / SCALE,
                                               score_bank[h % 2][:], ALU.mult, ALU.add).then_inc(scores_read, 1)
                if h % 2:
                    dve.wait_ge(scores_read, h + 1)
                    n = TT * (h - 1)
                    chained(nc.vector.tensor_reduce(small[:, 0, n:n + 4],
                                                    prob[:, h - 1:h + 1, :, :].rearrange("p h t n -> p (h t) n"),
                                                    X_AXIS, ALU.max))
                    nc.vector.scalar_tensor_tensor(
                        small[:, 1, n:n + 4].rearrange("p (h t) -> p h t", h=2),
                        small[:, 0, n:n + 4].rearrange("p (h t) -> p h t", h=2), -SCALE,
                        small[:, 5, h - 1:h + 1].unsqueeze(2).broadcast_to([P, 2, TT]),
                        ALU.mult, ALU.min).then_inc(neg_max_done, 1)

            def sinks():
                dve.wait_ge(neg_max_done, HEADS // 2)
                nc.vector.tensor_tensor(small[:, 3, :].rearrange("p (h t) -> p h t", h=HEADS),
                                        small[:, 1, :].rearrange("p (h t) -> p h t", h=HEADS),
                                        row[:, R_SINK:R_SINK + HEADS].unsqueeze(2).broadcast_to([P, HEADS, TT]),
                                        ALU.add).then_inc(sink_in, 1)

            def denominators():
                dve.wait_ge(exp_done, HEADS)
                dve.wait_ge(sink_exp, 1)
                chained(nc.vector.tensor_tensor(small[:, 6, :], small[:, 2, :], small[:, 4, :], ALU.add))
                chained(nc.vector.reciprocal(small[:, 7, :], small[:, 6, :]))

            def normalize(h):
                for t in range(TT):
                    ins = nc.vector.tensor_scalar(prob[:, h, t, :], prob[:, h, t, :],
                                                  small[:, 7, TT * h + t:TT * h + t + 1], None, ALU.mult)
                ins.then_inc(prob_ready, 1)

            def split_o(h):
                dve.wait_ge(o_hi_done, h + 1)
                nc.vector.tensor_tensor(a_lo[:, h, :], o_bank[h % 2][:, 0:SEQ], a_hi[:, h, :].bitcast(F32),
                                        ALU.subtract).then_inc(o_lo_done, 1)

            def layer_norm(n, lnr, s_rows, psum, ready):
                for t in range(TT):
                    for c in range(2):
                        v = xt[:, t, c * HALF:(c + 1) * HALF]
                        chained(nc.vector.scalar_tensor_tensor(v, v, ALPHA, psum[2 * t + c][:], ALU.mult, ALU.add))
                        ins = nc.vector.bn_stats(stat[:, t, c, :], v)
                    chained(ins)
                    nc.vector.bn_aggr(mv[:, t, 0:2], stat[:, t, :, :]).then_inc(ln_var, 1)
                if n == 0:
                    dve.wait_ge(s_rows, 16)
                for t in range(TT):
                    v = xt[:, t, :]
                    dve.wait_ge(ln_std, TT * n + t + 1)
                    chained(nc.vector.reciprocal(mv[:, t, 3:4], mv[:, t, 2:3]))
                    chained(nc.vector.tensor_scalar(v, v, mv[:, t, 0:1], mv[:, t, 3:4], ALU.subtract, ALU.mult))
                    chained(nc.vector.tensor_tensor(v, v, lnr[:, 0, :], ALU.mult))
                    nc.vector.tensor_tensor(v, v, lnr[:, 1, :], ALU.add).then_inc(ready, 1)

            dve.wait_ge(x_hi_done, 1)
            nc.vector.tensor_tensor(x_lo[:], xT_raw, x_hi[:].bitcast(F32), ALU.subtract).then_inc(x_lo_done, 1)
            for b in range(N_BLOCKS):
                if b == B_CONV + SPLIT:
                    some_taps(KT * CONV_WIDTH, KT)
                    dve.wait_ge(mean_done, 1)
                    nc.vector.tensor_tensor(acc, acc, bank[7][:, 0:SEQ].unsqueeze(1).broadcast_to([P, KT, SEQ]),
                                            ALU.subtract).then_inc(centered, 1)
                    dve.wait_ge(std_done, 1)
                    chained(nc.vector.reciprocal(sig[:, 1, :], sig[:, 0, :]))
                    dve.wait_ge(squared, 1)
                    for i in range(KT):
                        nc.vector.tensor_tensor(acc[:, i, :], acc[:, i, :], sig[:, 1, :], ALU.mult).then_inc(scaled, 1)
                        if i >= 1:
                            dve.wait_ge(c_hi_done, i)
                            nc.vector.tensor_tensor(x_lo[:, i - 1, :], acc[:, i - 1, :],
                                                    x_hi[:, i - 1, :].bitcast(F32), ALU.subtract).then_inc(c_lo_done, 1)
                    dve.wait_ge(c_hi_done, KT)
                    nc.vector.tensor_tensor(x_lo[:, KT - 1, :], acc[:, KT - 1, :],
                                            x_hi[:, KT - 1, :].bitcast(F32), ALU.subtract).then_inc(c_lo_done, 1)
                split_lo(b)
                if b == 2:
                    dve.wait_ge(consts_set, 4)
                    dve.wait_ge(s_par, 16)
                    dve.wait_ge(s_con, 16)
                    dve.wait_ge(s_row, 16)
                    chained(nc.vector.tensor_scalar(small[:, 5, 0:HEADS], row[:, R_SINK:R_SINK + HEADS], -1.0, None,
                                                    ALU.mult))
                if b % 2 and b >= 3 and (b - 3) // 2 < N_PAIRS:
                    evacuate((b - 3) // 2)
                if 30 <= b <= 33:
                    take_scores(2 * (b - 30))
                    take_scores(2 * (b - 30) + 1)
                    if b == 33:
                        sinks()
                if b == 35:
                    denominators()
                    dve.wait_ge(v_turned, 1)
                    for t in range(TT):
                        ins = nc.vector.tensor_copy(v_sb[:, t, :], o_bank[t][:])
                    ins.then_inc(v_copied, 1)
                if 35 <= b < 35 + HEADS:
                    normalize(b - 35)
                if 39 <= b < 39 + HEADS:
                    split_o(b - 39)
                if b < B_CONV:
                    some_taps(TAPS_PER_BLOCK, (b - 3) // 2 + 1 if b >= 3 else 0)
            dve.wait_ge(block_done, N_BLOCKS)
            dve.wait_ge(s_xt, 16)
            layer_norm(0, ln_rows, s_ln1, out_bank, x1_ready)
            for t in range(TT):
                dve.wait_ge(x1_hi_done, t + 1)
                nc.vector.tensor_tensor(x1_lo[:, t, :], xt[:, t, :], x1_hi[:, t, :].bitcast(F32),
                                        ALU.subtract).then_inc(x1_lo_done, 1)

            def per_token(col, n):
                return col.unsqueeze(2).broadcast_to([P, TT, n])

            dve.wait_ge(logits_done, 1)
            chained(nc.vector.tensor_tensor(lg[:], bank[3][:, 0:TT * LOGITS].rearrange("p (t n) -> p t n", t=TT),
                                            row[:, R_BIAS:R_BIAS + LOGITS].unsqueeze(1).broadcast_to([P, TT, LOGITS]),
                                            ALU.add))
            g_log = lg[:, :, 0:GROUPS]
            chained(nc.vector.tensor_reduce(rs[:, 0, :], g_log, X_AXIS, ALU.max))
            nc.vector.tensor_tensor(rg[:, 1, :, :], g_log, per_token(rs[:, 0, :], GROUPS),
                                    ALU.subtract).then_inc(exp_in, 1)
            chained(nc.vector.tensor_tensor(rg[:, 0, :, :], g_log, per_token(rs[:, 0, :], GROUPS), ALU.is_equal))
            chained(nc.vector.tensor_tensor(rg[:, 0, :, :], rg[:, 0, :, :],
                                            rank4.unsqueeze(1).broadcast_to([P, TT, GROUPS]), ALU.mult))
            chained(nc.vector.tensor_reduce(rs[:, 1, :], rg[:, 0, :, :], X_AXIS, ALU.max))
            chained(nc.vector.tensor_tensor(rg[:, 3, :, :], rg[:, 0, :, :], per_token(rs[:, 1, :], GROUPS),
                                            ALU.is_equal))
            nc.vector.tensor_scalar(rg[:, 0, :, :], rg[:, 3, :, :], NEVER, -NEVER, ALU.mult, ALU.add)
            e_log = lg[:, :, GROUPS:].rearrange("p t (g e) -> p t g e", g=GROUPS)

            def by_group(a):
                return a.unsqueeze(3).broadcast_to([P, TT, GROUPS, PER_GROUP])

            def grouped(a):
                return a.rearrange("p t (g e) -> p t g e", g=GROUPS)

            chained(nc.vector.tensor_tensor(grouped(rt[:, 0, :, :]), e_log, by_group(rg[:, 3, :, :]), ALU.mult))
            chained(nc.vector.tensor_tensor(grouped(rt[:, 1, :, :]), grouped(rt[:, 0, :, :]),
                                            by_group(rg[:, 0, :, :]), ALU.add))

            def first_of_largest(logit, one_hot, largest, key):
                chained(nc.vector.tensor_reduce(largest, logit, X_AXIS, ALU.max))
                chained(nc.vector.tensor_tensor(rt[:, 7, :, :], logit, per_token(largest, EXPERTS), ALU.is_equal))
                chained(nc.vector.tensor_tensor(rt[:, 7, :, :], rt[:, 7, :, :],
                                                rank32.unsqueeze(1).broadcast_to([P, TT, EXPERTS]), ALU.mult))
                chained(nc.vector.tensor_reduce(key, rt[:, 7, :, :], X_AXIS, ALU.max))
                chained(nc.vector.tensor_tensor(one_hot, rt[:, 7, :, :], per_token(key, EXPERTS), ALU.is_equal))

            first_of_largest(rt[:, 1, :, :], rt[:, 2, :, :], rs[:, 2, :], rs[:, 3, :])
            chained(nc.vector.scalar_tensor_tensor(rt[:, 3, :, :], rt[:, 2, :, :], -2 * NEVER, rt[:, 1, :, :],
                                                   ALU.mult, ALU.add))
            first_of_largest(rt[:, 3, :, :], rt[:, 4, :, :], rs[:, 4, :], rs[:, 5, :])
            nc.vector.tensor_tensor(rs[:, 7, :], rs[:, 4, :], rs[:, 2, :], ALU.subtract).then_inc(exp_in, 1)
            nc.vector.tensor_tensor(rt[:, 5, :, :], rt[:, 2, :, :], rt[:, 4, :, :], ALU.add).then_inc(onehot_done, 1)
            dve.wait_ge(router_exp, 2)
            chained(nc.vector.tensor_reduce(rs[:, 6, :], rg[:, 2, :, :], X_AXIS, ALU.add))
            chained(nc.vector.tensor_scalar(rs[:, 9, :], rs[:, 8, :], 1.0, None, ALU.add))
            chained(nc.vector.tensor_tensor(rs[:, 10, :], rs[:, 9, :], rs[:, 6, :], ALU.mult))
            chained(nc.vector.reciprocal(rs[:, 11, :], rs[:, 10, :]))
            chained(nc.vector.tensor_tensor(rs[:, 12, :], rs[:, 11, :], rs[:, 8, :], ALU.mult))
            nc.vector.tensor_tensor(rt[:, 2, :, :], rt[:, 2, :, :], per_token(rs[:, 11, :], EXPERTS), ALU.mult)
            dve.wait_ge(onehot_done, 1)
            chained(nc.vector.tensor_tensor(rt[:, 4, :, :], rt[:, 4, :, :], per_token(rs[:, 12, :], EXPERTS),
                                            ALU.mult))
            chained(nc.vector.tensor_tensor(rt[:, 6, :, :], rt[:, 2, :, :], rt[:, 4, :, :], ALU.add))
            dve.wait_ge(ranks_done, 1)
            chained(nc.vector.scalar_tensor_tensor(
                rt[:, 0, :, :], bank[4][:, 0:TT * EXPERTS].rearrange("p (t n) -> p t n", t=TT), 1.0,
                rt[:, 5, :, :], ALU.add, ALU.mult))
            chained(nc.vector.tensor_reduce(load_f[:], bank[5][0:1, 0:EXPERTS], X_AXIS, ALU.max))
            nc.vector.tensor_copy(load_i[:], load_f[:]).then_inc(load_known, 1)
            place = rt[:, 0, :, :]

            def build_gather(p, u):
                if from_pair(p, 2):
                    dve.wait_ge(sca_turned, p - 1)
                two = bass.ds(p * 2, 2)
                nc.vector.tensor_tensor(
                    gat[u].rearrange("p t (j s) -> p t j s", j=2),
                    iota.unsqueeze(1).unsqueeze(1).broadcast_to([P, TT, 2, WIN]),
                    place[:, :, two].unsqueeze(3).broadcast_to([P, TT, 2, WIN]), ALU.is_equal)
                nc.vector.tensor_copy(comb[u], rt[:, 6, :, two]).then_inc(gat_built, 1)

            def build_more(e, n, u):
                dve.wait_ge(sca_turned, n - 1)
                nc.vector.memset(sig[:, 0, 0:1], 0.0)
                for j in range(2):
                    nc.vector.tensor_copy(comb[u][:, :, j:j + 1], rt[:, 6, :, bass.ds(e, 1)])
                    ins = nc.vector.tensor_copy(more_place[:, :, j:j + 1], place[:, :, bass.ds(e, 1)])
                ins.then_inc(more_copied, 1)
                dve.wait_ge(more_copied, e * 2 + (u + 1))
                for j in range(2):
                    ins = nc.vector.scalar_tensor_tensor(
                        gat[u][:, :, j * WIN:(j + 1) * WIN],
                        iota.unsqueeze(1).broadcast_to([P, TT, WIN]), float(WIN * (1 + 2 * u + j)),
                        more_place[:, :, j:j + 1].broadcast_to([P, TT, WIN]), ALU.add, ALU.is_equal)
                ins.then_inc(gat_built, 1)

            def take_gate_up(p):
                dve.wait_ge(gu_done, 2 * p + 2)
                if from_pair(p, 1):
                    dve.wait_ge(h_summed, p)
                nc.vector.tensor_copy(gu[1], gu_bank[1][:]).then_inc(gu_copied1, 1)

            def gate_times_up(p):
                dve.wait_ge(moe_silu, p + 1)
                if from_pair(p, 1):
                    dve.wait_ge(down_done, 2 * p)
                nc.vector.tensor_tensor(hT, silu, h_bank[:].rearrange("p (j c n) -> p j c n", j=2, c=4)[:, :, HT:, :],
                                        ALU.mult).then_inc(h_ready, 1)

            def weigh_lo(p, u):
                for c in range(2):
                    dve.wait_ge(y_hi_done, 2 * p + (c + 1))
                    nc.vector.scalar_tensor_tensor(
                        y_lo[:, c * HALF:(c + 1) * HALF], y_bank[c][:], weight[u],
                        y_hi[:, c * HALF:(c + 1) * HALF].bitcast(F32), ALU.mult, ALU.subtract).then_inc(y_lo_done, 1)

            def pair(p, u, build=True):
                take_gate_up(p)
                if build:
                    build_gather(p + 2, u)
                gate_times_up(p)
                weigh_lo(p, u)

            build_gather(0, 0)
            build_gather(1, 1)
            for p in range(2):
                pair(p, p)
            with dve.Fori(1, PAIRS // 2 - 1) as i:
                for u in range(2):
                    pair(i * 2 + u, u)
            for p in range(PAIRS - 2, PAIRS):
                pair(p, p % 2, build=False)
            load = dve.value_load(load_i[0:1, 0:1], min_val=0, max_val=SEQ)
            with dve.If(load > WIN):
                with dve.Fori(0, EXPERTS) as e:
                    for u in range(2):
                        n = e * 2 + (PAIRS + u)
                        build_more(e, n, u)
                        take_gate_up(n)
                        gate_times_up(n)
                        weigh_lo(n, u)
                dve.wait_ge(scattered, PAIRS + 2 * EXPERTS)

            dve.wait_ge(scattered, PAIRS)
            dve.wait_ge(s_ln2, 16)
            layer_norm(1, ln2_rows, s_ln2, moe_bank, result)

        @block.tensor
        def _(pe):
            mm = nc.tensor.matmul

            def three_products(dst, pairs, first, last):
                (ah, al), (bh, bl) = pairs
                mm(dst, ah, bh, start=first, stop=False)
                mm(dst, ah, bl, start=False, stop=False)
                return mm(dst, al, bh, start=False, stop=last)

            def column_block(b, hi, lo, tile_ready=None):
                q = b // 2
                dst = pair_bank[q % PSUM_PAIRS][:, (b % 2) * SEQ:(b % 2 + 1) * SEQ]
                if b % 2 == 0 and q >= PSUM_PAIRS:
                    wait_pair_read(pe, q - PSUM_PAIRS)
                pe.wait_ge(w_lo_done, b + 1)
                for k in range(KT):
                    if tile_ready is not None:
                        pe.wait_ge(tile_ready, k + 1)
                    w = slice(k * P, (k + 1) * P)
                    ins = three_products(dst, ((w_hi[:, b % SPLIT, w], w_lo[:, b % SPLIT, w]),
                                               (hi[:, k, :], lo[:, k, :])), k == 0, k == KT - 1)
                ins.then_inc(block_done, 1)

            def scores(h):
                if h == 0:
                    pe.wait_ge(qkv_copied, (V_BLOCK - Q_BLOCK) // 2)
                if h >= 2:
                    pe.wait_ge(scores_read, h - 1)
                for t in range(TT):
                    ins = mm(score_bank[h % 2][:, t * SEQ:(t + 1) * SEQ], qT[:, h, t * P:(t + 1) * P],
                             kT[:, h // 2, :], start=True, stop=True)
                ins.then_inc(scores_done, 1)

            def turn_v():
                pe.wait_ge(qkv_copied, (GATE_BLOCK - Q_BLOCK) // 2)
                for t in range(TT):
                    for j in range(KV_HEADS):
                        ins = nc.tensor.transpose(o_bank[t][:, j * P:(j + 1) * P], vT[:, j, t * P:(t + 1) * P], ident)
                ins.then_inc(v_turned, 1)

            def turn_p(h):
                pe.wait_ge(prob_ready, h + 1)
                if h >= 1:
                    pe.wait_ge(p_copied, h)
                for kb in range(TT):
                    for t in range(TT):
                        ins = nc.tensor.transpose(t_bank[:, kb * SEQ + t * P:kb * SEQ + (t + 1) * P],
                                                  prob[:, h, t, kb * P:(kb + 1) * P], ident)
                ins.then_inc(p_turned, 1)

            def values(h):
                pe.wait_ge(p_copied, h + 1)
                if h == 0:
                    pe.wait_ge(v_copied, 1)
                if h >= 2:
                    pe.wait_ge(o_lo_done, h - 1)
                for kb in range(TT):
                    ins = mm(o_bank[h % 2][:, 0:SEQ], v_sb[:, kb, (h // 2) * P:(h // 2 + 1) * P],
                             pT[:, h % 2, kb, :], start=(kb == 0), stop=(kb == TT - 1))
                ins.then_inc(pv_done, 1)

            pe.wait_ge(x_lo_done, 1)
            for b in range(N_IN):
                if b == 24:
                    pe.wait_ge(s_con, 16)
                column_block(b, x_hi, x_lo)
                if 29 <= b <= 32:
                    scores(2 * (b - 29))
                    scores(2 * (b - 29) + 1)
                if b == 34:
                    turn_v()
                if 36 <= b < 36 + HEADS:
                    turn_p(b - 36)
                if 37 <= b < 37 + HEADS:
                    values(b - 37)
            for b in range(B_ATTN, B_CONV):
                column_block(b, a_hi, a_lo, o_lo_done if b == B_ATTN else None)
            pe.wait_ge(taps_done, KT * CONV_WIDTH)
            for i in range(KT):
                ins = mm(bank[7][:, 0:SEQ], mean_ones[:], acc[:, i, :], start=(i == 0), stop=(i == KT - 1))
            ins.then_inc(mean_done, 1)
            pe.wait_ge(squared, 1)
            for i in range(KT):
                ins = mm(bank[7][:, SEQ:], mean_ones[:], square[:, i, :], start=(i == 0), stop=(i == KT - 1))
            ins.then_inc(var_done, 1)
            for b in range(B_CONV, B_OUT):
                column_block(b, x_hi, x_lo, c_lo_done if b == B_CONV else None)
            for b in range(B_OUT, N_BLOCKS):
                k = b - B_OUT
                pe.wait_ge(w_lo_done, b + 1)
                pe.wait_ge(m_lo_done, k // 2 + 1)
                for t in range(TT):
                    for c in range(2):
                        n = slice(c * HALF, (c + 1) * HALF)
                        m = slice(t * P, (t + 1) * P)
                        ins = three_products(out_bank[2 * t + c][:], ((a_hi[:, k, m], a_lo[:, k, m]),
                                             (w_hi[:, b % SPLIT, n], w_lo[:, b % SPLIT, n])), k == 0, k == KT - 1)
                ins.then_inc(block_done, 1)

            for t in range(TT):
                pe.wait_ge(x1_ready, t + 1)
                for c in range(2):
                    dst = (pair_bank + [bank[7]])[2 * t + c]
                    for i in range(4):
                        ins = nc.tensor.transpose(dst[:, i * P:(i + 1) * P],
                                                  xt[:, t, (4 * c + i) * P:(4 * c + i + 1) * P], ident)
                    ins.then_inc(x1_turned, 1)
            pe.wait_ge(s_wr, 16)
            for t in range(TT):
                pe.wait_ge(x1T_copied, 2 * t + 2)
                for k in range(KT):
                    ins = mm(bank[3][:, t * LOGITS:(t + 1) * LOGITS], x1T[:, k, t * P:(t + 1) * P], wr[:, k, :],
                             start=(k == 0), stop=(k == KT - 1))
            ins.then_inc(logits_done, 1)
            one_hot = rt[:, 5, :, :]
            pe.wait_ge(onehot_done, 1)
            mm(bank[4][:, 0:EXPERTS], tri, one_hot[:, 0, :], start=True, stop=True)
            mm(bank[4][:, EXPERTS:2 * EXPERTS], ones[:], one_hot[:, 0, :], start=True, stop=False)
            mm(bank[4][:, EXPERTS:2 * EXPERTS], tri, one_hot[:, 1, :], start=False, stop=True)
            mm(bank[5][:, 0:EXPERTS], ones[:], one_hot[:, 0, :], start=True, stop=False)
            mm(bank[5][:, 0:EXPERTS], ones[:], one_hot[:, 1, :], start=False, stop=True).then_inc(ranks_done, 1)

            def gather(p, u, c):
                pe.wait_ge(gat_built, p + 1)
                if c:
                    pe.wait_ge(xg_copied, 2 * p + 1)
                elif from_pair(p, 1):
                    pe.wait_ge(sca_copied, p)
                for i in range(4):
                    n = slice((4 * c + i) * P, (4 * c + i + 1) * P)
                    dst = g_bank[:, i * P:(i + 1) * P]
                    for t in range(TT):
                        mm(dst, x1_hi[:, t, n], gat[u][:, t, :], start=(t == 0), stop=False)
                        ins = mm(dst, x1_lo[:, t, n], gat[u][:, t, :], start=False, stop=(t == TT - 1))
                ins.then_inc(gathered, 1)

            def scatter_matrix(p, u):
                pe.wait_ge(xg_copied, 2 * p + 2)
                g = gat[u].bitcast(F32)
                for t in range(TT):
                    nc.tensor.transpose(g_bank[:, t * P:(t + 1) * P], g[:, t, :], ident)
                for t in range(TT):
                    ins = mm(g_bank[:, SEQ:SEQ + 2], g[:, t, :], comb[u][:, t, :],
                             start=(t == 0), stop=(t == TT - 1))
                ins.then_inc(sca_turned, 1)

            def gate_up(p, u, j, slot):
                pe.wait_ge(xg_copied, 2 * p + 2)
                if from_pair(p, 1):
                    pe.wait_ge(y_lo_done, 2 * p + (j - 1))
                w = slots[:, slot, 0:GU_N].rearrange("p (k n) -> p k n", k=KT)
                for k in range(0, KT, 2):
                    for g in range(2):
                        ins = mm(gu_bank[j][g * WIN:(g + 1) * WIN, :], xg[u][:, k + g, j * WIN:(j + 1) * WIN],
                                 w[:, k + g, :], start=(k == 0), stop=(k == KT - 2))
                ins.then_inc(gu_done, 1)

            def sum_halves(p, j):
                pe.wait_ge(gu_copied1 if j else gu_copied0, p + 1)
                if j == 0 and from_pair(p, 1):
                    pe.wait_ge(h_ready, p)
                for c in range(2 * HT):
                    n = (j * 2 * HT + c) * WIN
                    ins = mm(h_bank[:, n:n + WIN], gu[j][:, c * P:(c + 1) * P], sel, start=True, stop=True)
                if j:
                    ins.then_inc(h_summed, 1)

            def down(p, slot):
                pe.wait_ge(h_ready, p + 1)
                for c in range(2):
                    for k in range(HT):
                        for j in range(2):
                            w = slots[:, slot[j], GU_N:SLOT_N].rearrange("p (k n) -> p k n", k=HT)
                            ins = mm(y_bank[c][j * WIN:(j + 1) * WIN, :], hT[:, j, k, :],
                                     w[:, k, c * HALF:(c + 1) * HALF], start=(k == 0), stop=(k == HT - 1))
                    ins.then_inc(down_done, 1)

            def scatter(p, u, first=False):
                pe.wait_ge(y_lo_done, 2 * p + 2)
                for t in range(TT):
                    for c in range(2):
                        dst = moe_bank[2 * t + c][:]
                        s = sca[u][:, t * P:(t + 1) * P]
                        n = slice(c * HALF, (c + 1) * HALF)
                        mm(dst, s, y_hi[:, n], start=first, stop=False, skip_group_check=True)
                        ins = mm(dst, s, y_lo[:, n], start=False, stop=True, skip_group_check=True)
                ins.then_inc(scattered, 1)

            def pair(p, u, turn, last=False):
                for j in range(2):
                    pe.wait_ge(gu_loaded[2 * u + j], 16 * turn)
                    gate_up(p, u, j, 2 * u + j)
                    if not last:
                        gather(p + 1, 1 - u, j)
                for j in range(2):
                    sum_halves(p, j)
                if not last:
                    scatter_matrix(p + 1, 1 - u)
                if from_pair(p, 1):
                    scatter(p - 1, 1 - u, first=(isinstance(p, int) and p == 1))
                for j in range(2):
                    pe.wait_ge(wd_loaded[2 * u + j], 16 * turn)
                down(p, (2 * u, 2 * u + 1))

            pe.wait_ge(x1_lo_done, TT)
            pe.wait_ge(load_known, 1)
            gather(0, 0, 0)
            gather(0, 0, 1)
            scatter_matrix(0, 0)
            for p in range(2):
                pair(p, p, 1)
            with pe.Fori(1, PAIRS // 2 - 1) as i:
                for u in range(2):
                    pair(i * 2 + u, u, i + 1)
            for p in range(PAIRS - 2, PAIRS):
                pair(p, p % 2, PAIRS // 2, last=(p == PAIRS - 1))
            scatter(PAIRS - 1, 1)

            load = pe.value_load(load_i[0:1, 0:1], min_val=0, max_val=SEQ)
            with pe.If(load > WIN):
                with pe.Fori(0, EXPERTS) as e:
                    pe.wait_ge(more_loaded, e * 32 + 32)
                    for u in range(2):
                        n = e * 2 + (PAIRS + u)
                        gather(n, u, 0)
                        gather(n, u, 1)
                        scatter_matrix(n, u)
                        gate_up(n, u, 0, 0)
                        gate_up(n, u, 1, 0)
                        sum_halves(n, 0)
                        sum_halves(n, 1)
                        down(n, (0, 0))
                        scatter(n, u)


def kernel(x, w_in, b_gate, w_dw, b_dw, conv_ln_g, conv_ln_b, w_conv_proj, attn_sink, w_attn_proj, w_out,
           ln1_g, ln1_b, w_router_group, b_router_group, w_router_expert, b_router_expert, w_gate_up, w_down,
           ln2_g, ln2_b):
    import concourse.bacc as bacc
    from concourse.bass_utils import run_bass_kernel_spmd

    def blocks(w, n):
        return w.reshape(KT, P, n, P).transpose(2, 1, 0, 3).reshape(n, P, KT * P)

    def channels(v):
        return v.reshape(KT, P, -1).transpose(1, 0, 2).reshape(P, -1)

    given = {k: np.asarray(v) for k, v in dict(
        x=x, w_in=w_in, b_gate=b_gate, w_dw=w_dw, b_dw=b_dw, g=conv_ln_g, b=conv_ln_b, w_conv=w_conv_proj,
        sink=attn_sink, w_attn=w_attn_proj, w_out=w_out, ln1_g=ln1_g, ln1_b=ln1_b, rg=w_router_group,
        brg=b_router_group, re=w_router_expert, bre=b_router_expert, gu=w_gate_up, wd=w_down, ln2_g=ln2_g,
        ln2_b=ln2_b).items()}
    g = {k: v[0] for k, v in given.items()}
    arrays = {
        "xT": g["x"].T.reshape(KT, P, SEQ).transpose(1, 0, 2),
        "x": g["x"],
        "consts": constants(),
        "chan": np.concatenate([g["b_gate"].reshape(2 * KT, P).T, channels(g["w_dw"].T), channels(g["b_dw"]),
                                channels(g["g"]), channels(g["b"])], axis=1),
        "rows": np.concatenate([g["brg"], g["bre"], g["sink"]])[None, :],
        "w_in": blocks(g["w_in"], N_IN),
        "w_attn": blocks(g["w_attn"], KT),
        "w_conv": blocks(g["w_conv"], KT),
        "w_out": g["w_out"],
        "ln1": np.stack([g["ln1_g"], g["ln1_b"]])[None],
        "ln2": np.stack([g["ln2_g"], g["ln2_b"]])[None],
        "w_router": np.concatenate([g["rg"], g["re"]], axis=1).reshape(KT, P, LOGITS).transpose(1, 0, 2),
        "w_gate_up": g["gu"].reshape(EXPERTS, KT, P, 2 * HIDDEN).transpose(0, 2, 1, 3).reshape(EXPERTS, P, GU_N),
        "w_down": g["wd"].reshape(EXPERTS, HT, P, D).transpose(0, 2, 1, 3).reshape(EXPERTS, P, WD_N),
    }
    nc = bacc.Bacc("TRN2", target_bir_lowering=False, num_devices=1)
    sent, args = {}, []
    for name, a in arrays.items():
        sent[f"in_{name}"] = np.ascontiguousarray(a)
        args.append(nc.dram_tensor(f"in_{name}", a.shape, F32, kind="ExternalInput").ap())
    out = nc.dram_tensor("out_x", (SEQ, D), F32, kind="ExternalOutput").ap()
    encoder_kernel(nc, *args, out)
    result = run_bass_kernel_spmd(nc, [sent], core_ids=[0])
    return result.results[0]["out_x"].reshape(1, SEQ, D)
```

```python
from contextlib import ExitStack

import concourse.bass as bass
import numpy as np
from concourse import mybir

F32 = mybir.dt.float32
F32R = mybir.dt.float32r
I32 = mybir.dt.int32
ALU = mybir.AluOpType
ACT = mybir.ActivationFunctionType
X_AXIS = mybir.AxisListType.X

P = 128
D = 1024
SEQ = 256
HEADS, KV_HEADS = 8, 4
CONV_WIDTH = 31
PAD = (CONV_WIDTH - 1) // 2
WINDOW = 128
GROUPS, PER_GROUP = 4, 8
EXPERTS = GROUPS * PER_GROUP
HIDDEN = D // 4
LN_EPS = 1e-5
ALPHA = 2.0 ** 0.25
SCALE = float(P) ** -0.5
FAR = 3e32
NEVER = 1e30

KT = D // P
TT = SEQ // P
HT = HIDDEN // P
LOGITS = GROUPS + EXPERTS
HALF = 512

ORDER = [c for i in range(KT) for c in (i, KT + i)]
ORDER += list(range(16, 32)) + list(range(40, 48)) + list(range(32, 40))
N_IN = len(ORDER)
B_ATTN, B_CONV, B_OUT = N_IN, N_IN + KT, N_IN + 2 * KT
N_BLOCKS = N_IN + 3 * KT
Q_BLOCK, V_BLOCK, GATE_BLOCK = 16, 28, 32
N_PAIRS = B_OUT // 2

RAW = 4
SPLIT = 2
PSUM_PAIRS = 3
TAPS_PER_BLOCK = 5

WIN = 64
PAIRS = EXPERTS // 2
WINDOWS = SEQ // WIN
ROUTED = 2 * SEQ
SLOTS = 4
GU_N = KT * 2 * HIDDEN
WD_N = HT * D
SLOT_N = GU_N + WD_N

C_IDENT, C_TRI, C_IOTA = 0, P, 2 * P
C_RANK4 = C_IOTA + ROUTED
C_RANK32 = C_RANK4 + GROUPS
C_TOKEN = C_RANK32 + EXPERTS
C_END = C_TOKEN + TT
A_BGATE = 0
A_WDW = 16
A_BDW = A_WDW + KT * CONV_WIDTH
A_LNG = A_BDW + KT
A_LNB = A_LNG + KT
A_END = A_LNB + KT
R_BIAS, R_SINK, R_END = 0, LOGITS, LOGITS + HEADS


def constants():
    c = np.zeros((P, C_END), np.float32)
    c[:, C_IDENT:C_IDENT + P] = np.eye(P)
    c[:, C_TRI:C_TRI + P] = np.arange(P)[:, None] < np.arange(P)[None, :]
    c[:, C_IOTA:C_IOTA + ROUTED] = np.arange(1, ROUTED + 1)
    c[:, C_RANK4:C_RANK4 + GROUPS] = np.arange(GROUPS, 0, -1)
    c[:, C_RANK32:C_RANK32 + EXPERTS] = np.arange(EXPERTS, 0, -1)
    c[:, C_TOKEN:C_TOKEN + TT] = 1 + np.arange(P)[:, None] + P * np.arange(TT)[None, :]
    return c


def distances():
    q = np.arange(P)[:, None, None] + P * np.arange(TT)[None, :, None]
    dist = np.abs(q - np.arange(SEQ)[None, None, :]).astype(np.float32)
    return np.where(dist <= WINDOW, dist, np.float32(FAR)).reshape(P, TT * SEQ)


def encoder_kernel(nc, xT, x, consts, dists, chan, rows, w_in, w_attn, w_conv, w_out, ln1, ln2, w_router,
                   w_gate_up, w_down, out):
    with ExitStack() as ctx:
        def sb(name, shape, dt=F32):
            return ctx.enter_context(nc.sbuf_tensor(name, shape, dt))

        def sem(name):
            return ctx.enter_context(nc.semaphore(name))

        slots = sb("slots", [P, SLOTS, SLOT_N])
        con = sb("con", [P, C_END])
        par = sb("par", [P, A_END])
        row = sb("row", [P, R_END])
        xt = sb("xt", [P, TT, D])
        raw = sb("raw", [P, RAW, D])
        gates = sb("gates", [P, 18, SEQ])
        kT = sb("kT", [P, KV_HEADS, SEQ])
        pT = sb("pT", [P, 2, TT, SEQ])
        sig = sb("sig", [P, 2, SEQ])
        wr = sb("wr", [P, KT, LOGITS])
        x_hi, x_lo = sb("x_hi", [P, KT, SEQ], F32R), sb("x_lo", [P, KT, SEQ], F32R)
        a_hi, a_lo = sb("a_hi", [P, KT, SEQ], F32R), sb("a_lo", [P, KT, SEQ], F32R)
        w_hi, w_lo = sb("w_hi", [P, SPLIT, D], F32R), sb("w_lo", [P, SPLIT, D], F32R)
        ones = sb("ones", [P, P])
        mean_ones = sb("mean_ones", [P, P])
        eps = sb("eps", [P, 1])
        small = sb("small", [P, 8, 2 * HEADS])
        stat = sb("stat", [P, TT, 2, 6])
        mv = sb("mv", [P, TT, 4])
        rt = sb("rt", [P, 10, TT, EXPERTS])
        rs = sb("rs", [P, 16, TT])
        rg = sb("rg", [P, 4, TT, GROUPS])
        lg = sb("lg", [P, TT, LOGITS])
        load_f = sb("load_f", [1, 1])
        load_i = sb("load_i", [1, 1], I32)
        starts_f = sb("starts_f", [1, WINDOWS + 1, EXPERTS])
        starts = sb("starts", [1, WINDOWS + 1, EXPERTS], I32)

        over = slots[:, 2:4, :].rearrange("p s n -> p (s n)")
        at = [0]

        def carve(n):
            at[0] += n
            return over[:, at[0] - n:at[0]]

        h_pad = carve(KT * (SEQ + 2 * PAD)).rearrange("p (i t) -> p i t", i=KT)
        acc = carve(KT * SEQ).rearrange("p (i t) -> p i t", i=KT)
        qT = carve(HEADS * SEQ).rearrange("p (i t) -> p i t", i=HEADS)
        v_sb = carve(TT * KV_HEADS * P).rearrange("p (t n) -> p t n", t=TT)
        prob = carve(HEADS * TT * SEQ).rearrange("p (h t n) -> p h t n", h=HEADS, t=TT)
        dist = carve(TT * SEQ)
        assert at[0] <= 2 * SLOT_N
        square = h_pad.rearrange("p i t -> p (i t)")[:, 0:KT * SEQ].rearrange("p (i t) -> p i t", i=KT)
        xT_raw = gates[:, 0:KT, :]
        ln_rows = gates[:, 0:8, :].rearrange("p (a b) t -> p a (b t)", a=2)
        vT = gates[:, 12:16, :]
        ln2_rows = raw[:, 2:4, :]
        x1T = raw[:, 0:2, :].rearrange("p a (b t) -> p (a b) t", t=SEQ)

        x1_hi = x_hi[:].rearrange("p i t -> p (i t)").rearrange("p (t n) -> p t n", t=TT)
        x1_lo = x_lo[:].rearrange("p i t -> p (i t)").rearrange("p (t n) -> p t n", t=TT)
        compact = w_hi[:, 1, :].rearrange("p (t n) -> p t n", t=TT)
        xgT = gates[:].rearrange("p a t -> p (a t)").rearrange("p (k n) -> p k n", k=KT)
        y_hi, y_lo = w_hi[:, 0, :], w_lo[:, 0, :]
        sca = [w_lo[:, 1, SEQ * i:SEQ * (i + 1)] for i in range(2)]
        xg = [raw[:, i, :].rearrange("p (k n) -> p k n", k=KT) for i in range(2)]
        gat = [pT[:, 0, i, :].rearrange("p (t n) -> p t n", t=TT) for i in range(2)]
        swished, h_sb = pT[:, 1, 0, :], pT[:, 1, 1, :]
        hT = kT[:, 0, :].rearrange("p (k n) -> p k n", k=HT)
        info = [kT[:, 1, 16 * i:16 * i + 3 * TT].rearrange("p (t c) -> p t c", t=TT) for i in range(2)]
        token = [kT[:, 1, 32 + i:33 + i] for i in range(2)]
        weight = [kT[:, 1, 34 + i:35 + i] for i in range(2)]
        more_place = kT[:, 1, 40:40 + 2 * TT].rearrange("p (t j) -> p t j", t=TT)

        ident = con[:, C_IDENT:C_IDENT + P]
        tri = con[:, C_TRI:C_TRI + P]
        iota = con[:, C_IOTA:C_IOTA + ROUTED]
        rank4 = con[:, C_RANK4:C_RANK4 + GROUPS]
        rank32 = con[:, C_RANK32:C_RANK32 + EXPERTS]

        bank = [ctx.enter_context(nc.psum_tensor(f"bank{i}", [P, HALF], F32)) for i in range(8)]
        pair_bank = bank[0:3]
        score_bank = bank[3:5]
        t_bank, o_bank = bank[5], [bank[6], bank[7]]
        out_bank = [bank[3], bank[4], bank[5], bank[6]]
        moe_bank = out_bank
        cmp_f = raw[:, 2, :].rearrange("p (t n) -> p t n", t=TT)
        gu_bank, y_bank, t7_bank = bank[0], [bank[1], bank[2]], bank[7]
        free_bank = [bank[0], bank[1], bank[2], bank[7]]

        s_xT, s_con, s_par, s_row, s_xt = (sem(n) for n in ("s_xT", "s_con", "s_par", "s_row", "s_xt"))
        s_ln1, s_ln2, s_wr, s_out = (sem(n) for n in ("s_ln1", "s_ln2", "s_wr", "s_out"))
        raw_loaded = [sem(f"raw_loaded{i}") for i in range(RAW)]
        gu_loaded = [sem(f"gu_loaded{i}") for i in range(SLOTS)]
        wd_loaded = [sem(f"wd_loaded{i}") for i in range(SLOTS)]
        consts_set = sem("consts_set")
        x_hi_done, x_lo_done = sem("x_hi_done"), sem("x_lo_done")
        w_hi_done, w_lo_done = sem("w_hi_done"), sem("w_lo_done")
        block_done = sem("block_done")
        sigmoid_done, glu_done = sem("sigmoid_done"), sem("glu_done")
        qkv_copied, gates_done = sem("qkv_copied"), sem("gates_done")
        taps_done = sem("taps_done")
        scores_done, scores_read, row_max_done = sem("scores_done"), sem("scores_read"), sem("row_max_done")
        neg_max_done, exp_done, sink_in, sink_exp = (sem(n) for n in ("neg_max_done", "exp_done", "sink_in", "sink_exp"))
        v_turned, v_copied = sem("v_turned"), sem("v_copied")
        prob_ready, p_turned, p_copied = sem("prob_ready"), sem("p_turned"), sem("p_copied")
        pv_done, o_hi_done, o_lo_done = sem("pv_done"), sem("o_hi_done"), sem("o_lo_done")
        attn_gated, conv_gated, merged = sem("attn_gated"), sem("conv_gated"), sem("merged")
        m_hi_done, m_lo_done = sem("m_hi_done"), sem("m_lo_done")
        mean_done, centered, squared, var_done = (sem(n) for n in ("mean_done", "centered", "squared", "var_done"))
        std_done, scaled, silu_done, c_hi_done, c_lo_done = (
            sem(n) for n in ("std_done", "scaled", "silu_done", "c_hi_done", "c_lo_done"))
        dve_step = sem("dve_step")
        ln_var, ln_std, x1_ready, x1_hi_done, x1_lo_done = (
            sem(n) for n in ("ln_var", "ln_std", "x1_ready", "x1_hi_done", "x1_lo_done"))
        x1_turned, x1T_copied, logits_done = sem("x1_turned"), sem("x1T_copied"), sem("logits_done")
        exp_in, router_exp, onehot_done, ranks_done, route_done, load_known = (
            sem(n) for n in ("exp_in", "router_exp", "onehot_done", "ranks_done", "route_done", "load_known"))
        s_dist = sem("s_dist")
        compact_built, gathered, xgT_even, xgT_odd, pads_set = (
            sem(n) for n in ("compact_built", "gathered", "xgT_even", "xgT_odd", "pads_set"))
        xg_ready, gat_built, info_done, info_copied, sca_built = (
            sem(n) for n in ("xg_ready", "gat_built", "info_done", "info_copied", "sca_built"))
        gu_done, swish_done, h_ready, h_turned, hT_copied = (
            sem(n) for n in ("gu_done", "swish_done", "h_ready", "h_turned", "hT_copied"))
        down_done, y_hi_done, y_lo_done, scattered = (
            sem(n) for n in ("down_done", "y_hi_done", "y_lo_done", "scattered"))
        more_loaded, more_copied = sem("more_loaded"), sem("more_copied")
        result = sem("result")

        def from_pair(p, n):
            return not isinstance(p, int) or p >= n

        def block_of(b):
            if b < B_ATTN:
                return w_in[ORDER[b]]
            if b < B_CONV:
                return w_attn[b - B_ATTN]
            if b < B_OUT:
                return w_conv[b - B_CONV]
            return w_out[(b - B_OUT) * P:(b - B_OUT + 1) * P, :]

        def wait_pair_read(eng, q):
            if q < Q_BLOCK // 2:
                eng.wait_ge(glu_done, q + 1)
            elif q < GATE_BLOCK // 2:
                eng.wait_ge(qkv_copied, q - Q_BLOCK // 2 + 1)
            elif q < N_IN // 2:
                eng.wait_ge(gates_done, q - GATE_BLOCK // 2 + 1)
            elif q < B_CONV // 2:
                eng.wait_ge(attn_gated, q - N_IN // 2 + 1)
            else:
                eng.wait_ge(conv_gated, q - B_CONV // 2 + 1)

        def last_head_step(h):
            return 38 + h

        block = ctx.enter_context(nc.Block())

        @block.sync
        def _(sp):
            def load_gate_up(e):
                sp.dma_start(slots[:, e % SLOTS, 0:GU_N], w_gate_up[e]).then_inc(gu_loaded[e % SLOTS], 16)

            def load_down(e):
                sp.dma_start(slots[:, e % SLOTS, GU_N:SLOT_N], w_down[e]).then_inc(wd_loaded[e % SLOTS], 16)

            sp.dma_start(xT_raw, xT).then_inc(s_xT, 16)
            for b in range(N_BLOCKS):
                if b >= RAW:
                    sp.wait_ge(w_lo_done, b - RAW + 1)
                sp.dma_start(raw[:, b % RAW, :], block_of(b)).then_inc(raw_loaded[b % RAW], 16)
                if b == 2:
                    sp.dma_start(par[:], chan).then_inc(s_par, 16)
                    sp.dma_start(con[:], consts).then_inc(s_con, 16)
                    sp.dma_start(dist, dists).then_inc(s_dist, 16)
                    sp.dma_start(row[:], rows.broadcast_to([P, R_END])).then_inc(s_row, 16)
                if b == 10:
                    load_gate_up(0)
                if b == 14:
                    load_gate_up(1)
                if b == 18:
                    load_down(0)
                    load_down(1)
                if b == 22:
                    sp.dma_start(xt[:], x.rearrange("(t p) n -> p t n", p=P)).then_inc(s_xt, 16)
                    sp.dma_start(wr[:], w_router).then_inc(s_wr, 16)
                if b == B_OUT + RAW:
                    sp.wait_ge(silu_done, KT)
                    sp.wait_ge(pv_done, HEADS)
                    load_gate_up(2)
                if b == B_OUT + RAW + 2:
                    load_gate_up(3)
            load_down(2)
            load_down(3)
            sp.wait_ge(m_lo_done, KT // 2)
            sp.dma_start(ln_rows, ln1.broadcast_to([P, 2, D])).then_inc(s_ln1, 16)
            sp.wait_ge(load_known, 1)
            sp.dma_start(ln2_rows, ln2.broadcast_to([P, 2, D])).then_inc(s_ln2, 16)
            load = sp.value_load(load_i[0:1, 0:1], min_val=0, max_val=SEQ)
            with sp.Fori(1, EXPERTS // SLOTS) as i:
                for s in range(SLOTS):
                    e = i * SLOTS + s
                    if s % 2 == 0:
                        sp.wait_ge(gu_done, i * 2 + (s // 2 - 1))
                    sp.dma_start(slots[:, s, 0:GU_N], w_gate_up[e]).then_inc(gu_loaded[s], 16)
                    if s % 2:
                        sp.wait_ge(down_done, i * 4 + (s // 2 * 2 - 2))
                        for r in (s - 1, s):
                            sp.dma_start(slots[:, r, GU_N:SLOT_N], w_down[i * SLOTS + r]).then_inc(wd_loaded[r], 16)
            with sp.If(load > WIN):
                with sp.Fori(0, EXPERTS) as e:
                    sp.wait_ge(scattered, e * 2 + PAIRS)
                    sp.dma_start(slots[:, 0, 0:GU_N], w_gate_up[e]).then_inc(more_loaded, 16)
                    sp.dma_start(slots[:, 0, GU_N:SLOT_N], w_down[e]).then_inc(more_loaded, 16)
            for t in range(TT):
                sp.wait_ge(result, t + 1)
                sp.dma_start(out[t * P:(t + 1) * P, :], xt[:, t, :]).then_inc(s_out, 16)
            sp.wait_ge(s_out, 16 * TT)

        @block.gpsimd
        def _(pool):
            nc.gpsimd.memset(h_pad, 0.0).then_inc(consts_set, 1)
            nc.gpsimd.memset(ones[:], 1.0).then_inc(consts_set, 1)
            nc.gpsimd.memset(mean_ones[:], 1.0 / D).then_inc(consts_set, 1)
            nc.gpsimd.memset(eps[:], LN_EPS).then_inc(consts_set, 1)

            pool.wait_ge(x1_ready, TT)
            nc.gpsimd.memset(xgT[:, :, ROUTED:], 0.0).then_inc(pads_set, 1)

            def take_tokens(u, first, second):
                for j, w in enumerate((first, second)):
                    at = pool.value_load(starts[0:1, w[0], w[1]], min_val=0, max_val=ROUTED)
                    ins = nc.gpsimd.tensor_copy(xg[u][:, :, j * WIN:(j + 1) * WIN], xgT[:, :, bass.ds(at, WIN)])
                ins.then_inc(xg_ready, 1)

            pool.wait_ge(load_known, 1)
            pool.wait_ge(pads_set, 1)
            pool.wait_ge(xgT_even, KT // 2)
            pool.wait_ge(xgT_odd, KT // 2)
            for p in range(2):
                take_tokens(p, (0, bass.ds(2 * p, 1)), (0, bass.ds(2 * p + 1, 1)))
            with pool.Fori(1, PAIRS // 2) as i:
                for u in range(2):
                    pool.wait_ge(gu_done, i * 2 + (u - 1))
                    take_tokens(u, (0, bass.ds(i * 4 + 2 * u, 1)), (0, bass.ds(i * 4 + (2 * u + 1), 1)))
            load = pool.value_load(load_i[0:1, 0:1], min_val=0, max_val=SEQ)
            with pool.If(load > WIN):
                with pool.Fori(0, EXPERTS) as e:
                    for u in range(2):
                        pool.wait_ge(gu_done, e * 2 + (PAIRS + u - 1))
                        take_tokens(u, (1 + 2 * u, bass.ds(e, 1)), (2 + 2 * u, bass.ds(e, 1)))

        @block.scalar
        def _(act):
            def split_hi(b):
                act.wait_ge(raw_loaded[b % RAW], 16 * (b // RAW + 1))
                if b >= SPLIT:
                    act.wait_ge(block_done, b - SPLIT + 1)
                nc.scalar.copy(w_hi[:, b % SPLIT, :], raw[:, b % RAW, :]).then_inc(w_hi_done, 1)

            def evacuate(q):
                src = pair_bank[q % PSUM_PAIRS]
                act.wait_ge(block_done, 2 * q + 2)
                if q < Q_BLOCK // 2:
                    if q >= 2:
                        act.wait_ge(glu_done, q - 1)
                    nc.scalar.activation(sig[:, q % 2, :], src[:, SEQ:], ACT.Sigmoid).then_inc(sigmoid_done, 1)
                elif q < GATE_BLOCK // 2:
                    n = 2 * (q - Q_BLOCK // 2)
                    dst = qT[:, n:n + 2, :] if n < HEADS else (
                        kT[:, n - 8:n - 6, :] if n < 12 else vT[:, n - 12:n - 10, :])
                    nc.scalar.copy(dst, src[:].rearrange("p (a t) -> p a t", a=2)).then_inc(qkv_copied, 1)
                elif q < N_IN // 2:
                    if q == GATE_BLOCK // 2:
                        act.wait_ge(s_par, 16)
                        act.wait_ge(x_lo_done, 1)
                    if q == GATE_BLOCK // 2 + 2:
                        act.wait_ge(v_turned, 1)
                    for j in range(2):
                        c = ORDER[2 * q + j] - GATE_BLOCK
                        ins = nc.scalar.activation(gates[:, c, :], src[:, j * SEQ:(j + 1) * SEQ], ACT.Sigmoid,
                                                   bias=par[:, A_BGATE + c:A_BGATE + c + 1])
                    ins.then_inc(gates_done, 1)
                elif q >= B_CONV // 2:
                    m = q - B_CONV // 2
                    act.wait_ge(merged, m + 1)
                    nc.scalar.copy(a_hi[:, 2 * m:2 * m + 2, :], gates[:, 2 * m:2 * m + 2, :]).then_inc(m_hi_done, 1)

            def exponentials(h):
                act.wait_ge(neg_max_done, h // 2 + 1)
                for t in range(TT):
                    ins = nc.scalar.activation(prob[:, h, t, :], prob[:, h, t, :], ACT.Exp, scale=SCALE,
                                               bias=small[:, 1, TT * h + t:TT * h + t + 1],
                                               accum_out=small[:, 2, TT * h + t:TT * h + t + 1])
                ins.then_inc(exp_done, 1)

            def copy_pT(h):
                act.wait_ge(p_turned, h + 1)
                if h >= 2:
                    act.wait_ge(pv_done, h - 1)
                nc.scalar.copy(pT[:, h % 2, :, :], t_bank[:].rearrange("p (a t) -> p a t", a=2)).then_inc(p_copied, 1)

            def split_o(h):
                act.wait_ge(pv_done, h + 1)
                nc.scalar.copy(a_hi[:, h, :], o_bank[h % 2][:, 0:SEQ]).then_inc(o_hi_done, 1)

            act.wait_ge(s_xT, 16)
            nc.scalar.copy(x_hi[:], xT_raw).then_inc(x_hi_done, 1)
            for b in range(N_BLOCKS):
                if b == B_CONV + SPLIT:
                    act.wait_ge(centered, 1)
                    nc.scalar.activation(square, acc, ACT.Square).then_inc(squared, 1)
                    act.wait_ge(var_done, 1)
                    act.wait_ge(consts_set, 4)
                    nc.scalar.activation(sig[:, 0, :], bank[7][:, SEQ:], ACT.Sqrt, bias=eps[:, 0:1]).then_inc(std_done, 1)
                    act.wait_ge(x_lo_done, 1)
                    for i in range(KT):
                        act.wait_ge(scaled, i + 1)
                        nc.scalar.activation(acc[:, i, :], acc[:, i, :], ACT.Silu,
                                             scale=par[:, A_LNG + i:A_LNG + i + 1],
                                             bias=par[:, A_LNB + i:A_LNB + i + 1]).then_inc(silu_done, 1)
                        act.wait_ge(silu_done, i + 1)
                        if i == 0:
                            act.wait_ge(block_done, N_IN)
                        nc.scalar.copy(x_hi[:, i, :], acc[:, i, :]).then_inc(c_hi_done, 1)
                split_hi(b)
                if b % 2 and b >= 3:
                    q = (b - 3) // 2
                    if q < N_PAIRS:
                        evacuate(q)
                if 31 <= b <= 34:
                    for h in (2 * (b - 31), 2 * (b - 31) + 1):
                        exponentials(h)
                    if b == 34:
                        act.wait_ge(sink_in, 1)
                        nc.scalar.activation(small[:, 4, :], small[:, 3, :], ACT.Exp).then_inc(sink_exp, 1)
                if 38 <= b < 38 + HEADS:
                    copy_pT(b - 38)
                if 39 <= b < 39 + HEADS:
                    split_o(b - 39)

            for t in range(TT):
                act.wait_ge(ln_var, t + 1)
                nc.scalar.activation(mv[:, t, 2:3], mv[:, t, 1:2], ACT.Sqrt, bias=eps[:, 0:1]).then_inc(ln_std, 1)
            for t in range(TT):
                act.wait_ge(x1_ready, t + 1)
                nc.scalar.copy(x1_hi[:, t, :], xt[:, t, :]).then_inc(x1_hi_done, 1)
                for c in range(2):
                    act.wait_ge(x1_turned, 2 * t + c + 1)
                    src = (pair_bank + [bank[7]])[2 * t + c]
                    nc.scalar.copy(x1T[:, 4 * c:4 * c + 4, t * P:(t + 1) * P],
                                   src[:].rearrange("p (a t) -> p a t", a=4)).then_inc(x1T_copied, 1)
            act.wait_ge(exp_in, 1)
            nc.scalar.activation(rg[:, 2, :, :], rg[:, 1, :, :], ACT.Exp).then_inc(router_exp, 1)
            act.wait_ge(exp_in, 2)
            nc.scalar.activation(rs[:, 8, :], rs[:, 7, :], ACT.Exp).then_inc(router_exp, 1)

            for k in range(0, KT, 2):
                act.wait_ge(gathered, k + 1)
                nc.scalar.copy(xgT[:, k, 0:ROUTED], free_bank[k % 4][:]).then_inc(xgT_even, 1)

            def copy_info(p, u):
                act.wait_ge(info_done, p + 1)
                if from_pair(p, 2):
                    act.wait_ge(h_ready, p - 1)
                    act.wait_ge(sca_built, p - 1)
                nc.scalar.copy(token[u], t7_bank[:, 0:1])
                for j in range(2):
                    ins = nc.scalar.copy(weight[u][j * WIN:(j + 1) * WIN, :],
                                         t7_bank[j * WIN:(j + 1) * WIN, 1 + j:2 + j])
                ins.then_inc(info_copied, 1)

            def swish(p):
                act.wait_ge(gu_done, p + 1)
                if from_pair(p, 1):
                    act.wait_ge(h_ready, p)
                nc.scalar.activation(swished, gu_bank[:, 0:HIDDEN], ACT.Silu).then_inc(swish_done, 1)

            def copy_hT(p):
                act.wait_ge(h_turned, p + 1)
                if from_pair(p, 1):
                    act.wait_ge(down_done, 2 * p)
                nc.scalar.copy(hT, t7_bank[:, 0:HT * P].rearrange("p (k n) -> p k n", k=HT)).then_inc(hT_copied, 1)

            def split_y_hi(p):
                for c in range(2):
                    act.wait_ge(down_done, 2 * p + (c + 1))
                    if c == 0 and from_pair(p, 1):
                        act.wait_ge(scattered, p)
                    nc.scalar.copy(y_hi[:, c * HALF:(c + 1) * HALF], y_bank[c][:]).then_inc(y_hi_done, 1)

            def pair(p, u, last=False):
                swish(p)
                copy_hT(p)
                split_y_hi(p)
                if not last:
                    copy_info(p + 1, 1 - u)

            copy_info(0, 0)
            for p in range(2):
                pair(p, p)
            with act.Fori(1, PAIRS // 2 - 1) as i:
                for u in range(2):
                    pair(i * 2 + u, u)
            for p in range(PAIRS - 2, PAIRS):
                pair(p, p % 2, last=(p == PAIRS - 1))
            load = act.value_load(load_i[0:1, 0:1], min_val=0, max_val=SEQ)
            with act.If(load > WIN):
                with act.Fori(0, EXPERTS) as e:
                    for u in range(2):
                        n = e * 2 + (PAIRS + u)
                        copy_info(n, u)
                        swish(n)
                        copy_hT(n)
                        split_y_hi(n)
            for t in range(TT):
                act.wait_ge(ln_var, TT + t + 1)
                nc.scalar.activation(mv[:, t, 2:3], mv[:, t, 1:2], ACT.Sqrt, bias=eps[:, 0:1]).then_inc(ln_std, 1)

        @block.vector
        def _(dve):
            steps = [0]

            def chained(ins):
                steps[0] += 1
                ins.then_inc(dve_step, 1)
                dve.wait_ge(dve_step, steps[0])

            def split_lo(b):
                dve.wait_ge(w_hi_done, b + 1)
                nc.vector.tensor_tensor(w_lo[:, b % SPLIT, :], raw[:, b % RAW, :],
                                        w_hi[:, b % SPLIT, :].bitcast(F32), ALU.subtract).then_inc(w_lo_done, 1)

            def conv_taps():
                n = 0
                for m in range(0, KT, 2):
                    for tap in range(CONV_WIDTH):
                        for i in (m, m + 1):
                            w = par[:, A_WDW + i * CONV_WIDTH + tap:A_WDW + i * CONV_WIDTH + tap + 1]
                            h = h_pad[:, i, tap:tap + SEQ]
                            if tap:
                                dve.wait_ge(taps_done, n - 1)
                                ins = nc.vector.scalar_tensor_tensor(acc[:, i, :], h, w, acc[:, i, :], ALU.mult, ALU.add)
                            else:
                                ins = nc.vector.tensor_scalar(acc[:, i, :], h, w, par[:, A_BDW + i:A_BDW + i + 1],
                                                              ALU.mult, ALU.add)
                            ins.then_inc(taps_done, 1)
                            n += 1
                            yield m

            taps = conv_taps()
            done = [0]

            def some_taps(count, ready):
                for _ in range(count):
                    m = done[0] // (2 * CONV_WIDTH) * 2
                    if m + 2 > ready or done[0] >= KT * CONV_WIDTH:
                        return
                    next(taps)
                    done[0] += 1

            def evacuate(q):
                src = pair_bank[q % PSUM_PAIRS]
                if q < Q_BLOCK // 2:
                    dve.wait_ge(sigmoid_done, q + 1)
                    nc.vector.tensor_tensor(h_pad[:, q, PAD:PAD + SEQ], src[:, 0:SEQ], sig[:, q % 2, :],
                                            ALU.mult).then_inc(glu_done, 1)
                    dve.wait_ge(glu_done, q + 1)
                elif N_IN // 2 <= q < B_CONV // 2:
                    m = q - N_IN // 2
                    dve.wait_ge(block_done, 2 * q + 2)
                    dve.wait_ge(gates_done, N_IN // 2 - GATE_BLOCK // 2)
                    g = gates[:, KT + 2 * m:KT + 2 * m + 2, :]
                    nc.vector.tensor_tensor(g, src[:].rearrange("p (a t) -> p a t", a=2), g,
                                            ALU.mult).then_inc(attn_gated, 1)
                elif q >= B_CONV // 2:
                    m = q - B_CONV // 2
                    g, other = gates[:, 2 * m:2 * m + 2, :], gates[:, KT + 2 * m:KT + 2 * m + 2, :]
                    dve.wait_ge(block_done, 2 * q + 2)
                    nc.vector.tensor_tensor(g, src[:].rearrange("p (a t) -> p a t", a=2), g,
                                            ALU.mult).then_inc(conv_gated, 1)
                    dve.wait_ge(conv_gated, m + 1)
                    dve.wait_ge(attn_gated, m + 1)
                    nc.vector.tensor_tensor(g, g, other, ALU.add).then_inc(merged, 1)
                    dve.wait_ge(m_hi_done, m + 1)
                    nc.vector.tensor_tensor(a_lo[:, 2 * m:2 * m + 2, :], g,
                                            a_hi[:, 2 * m:2 * m + 2, :].bitcast(F32),
                                            ALU.subtract).then_inc(m_lo_done, 1)

            def take_scores(h):
                dve.wait_ge(scores_done, h + 1)
                slope = 2.0 ** (-8.0 * (h + 1) / HEADS)
                nc.vector.scalar_tensor_tensor(prob[:, h, :, :].rearrange("p t n -> p (t n)"), dist, -slope / SCALE,
                                               score_bank[h % 2][:], ALU.mult, ALU.add).then_inc(scores_read, 1)
                if h % 2:
                    dve.wait_ge(scores_read, h + 1)
                    n = TT * (h - 1)
                    chained(nc.vector.tensor_reduce(small[:, 0, n:n + 4],
                                                    prob[:, h - 1:h + 1, :, :].rearrange("p h t n -> p (h t) n"),
                                                    X_AXIS, ALU.max))
                    nc.vector.scalar_tensor_tensor(
                        small[:, 1, n:n + 4].rearrange("p (h t) -> p h t", h=2),
                        small[:, 0, n:n + 4].rearrange("p (h t) -> p h t", h=2), -SCALE,
                        small[:, 5, h - 1:h + 1].unsqueeze(2).broadcast_to([P, 2, TT]),
                        ALU.mult, ALU.min).then_inc(neg_max_done, 1)

            def sinks():
                dve.wait_ge(neg_max_done, HEADS // 2)
                nc.vector.tensor_tensor(small[:, 3, :].rearrange("p (h t) -> p h t", h=HEADS),
                                        small[:, 1, :].rearrange("p (h t) -> p h t", h=HEADS),
                                        row[:, R_SINK:R_SINK + HEADS].unsqueeze(2).broadcast_to([P, HEADS, TT]),
                                        ALU.add).then_inc(sink_in, 1)

            def denominators():
                dve.wait_ge(exp_done, HEADS)
                dve.wait_ge(sink_exp, 1)
                chained(nc.vector.tensor_tensor(small[:, 6, :], small[:, 2, :], small[:, 4, :], ALU.add))
                chained(nc.vector.reciprocal(small[:, 7, :], small[:, 6, :]))

            def normalize(h):
                for t in range(TT):
                    ins = nc.vector.tensor_scalar(prob[:, h, t, :], prob[:, h, t, :],
                                                  small[:, 7, TT * h + t:TT * h + t + 1], None, ALU.mult)
                ins.then_inc(prob_ready, 1)

            def split_o(h):
                dve.wait_ge(o_hi_done, h + 1)
                nc.vector.tensor_tensor(a_lo[:, h, :], o_bank[h % 2][:, 0:SEQ], a_hi[:, h, :].bitcast(F32),
                                        ALU.subtract).then_inc(o_lo_done, 1)

            def layer_norm(n, lnr, s_rows, psum, ready):
                for t in range(TT):
                    for c in range(2):
                        v = xt[:, t, c * HALF:(c + 1) * HALF]
                        chained(nc.vector.scalar_tensor_tensor(v, v, ALPHA, psum[2 * t + c][:], ALU.mult, ALU.add))
                        ins = nc.vector.bn_stats(stat[:, t, c, :], v)
                    chained(ins)
                    nc.vector.bn_aggr(mv[:, t, 0:2], stat[:, t, :, :]).then_inc(ln_var, 1)
                if n == 0:
                    dve.wait_ge(s_rows, 16)
                for t in range(TT):
                    v = xt[:, t, :]
                    dve.wait_ge(ln_std, TT * n + t + 1)
                    chained(nc.vector.reciprocal(mv[:, t, 3:4], mv[:, t, 2:3]))
                    chained(nc.vector.scalar_tensor_tensor(v, v, mv[:, t, 0:1], lnr[:, 0, :], ALU.subtract, ALU.mult))
                    nc.vector.scalar_tensor_tensor(v, v, mv[:, t, 3:4], lnr[:, 1, :], ALU.mult,
                                                   ALU.add).then_inc(ready, 1)

            dve.wait_ge(x_hi_done, 1)
            nc.vector.tensor_tensor(x_lo[:], xT_raw, x_hi[:].bitcast(F32), ALU.subtract).then_inc(x_lo_done, 1)
            for b in range(N_BLOCKS):
                if b == B_CONV + SPLIT:
                    some_taps(KT * CONV_WIDTH, KT)
                    dve.wait_ge(mean_done, 1)
                    nc.vector.tensor_tensor(acc, acc, bank[7][:, 0:SEQ].unsqueeze(1).broadcast_to([P, KT, SEQ]),
                                            ALU.subtract).then_inc(centered, 1)
                    dve.wait_ge(std_done, 1)
                    chained(nc.vector.reciprocal(sig[:, 1, :], sig[:, 0, :]))
                    dve.wait_ge(squared, 1)
                    for i in range(KT):
                        nc.vector.tensor_tensor(acc[:, i, :], acc[:, i, :], sig[:, 1, :], ALU.mult).then_inc(scaled, 1)
                        if i >= 1:
                            dve.wait_ge(c_hi_done, i)
                            nc.vector.tensor_tensor(x_lo[:, i - 1, :], acc[:, i - 1, :],
                                                    x_hi[:, i - 1, :].bitcast(F32), ALU.subtract).then_inc(c_lo_done, 1)
                    dve.wait_ge(c_hi_done, KT)
                    nc.vector.tensor_tensor(x_lo[:, KT - 1, :], acc[:, KT - 1, :],
                                            x_hi[:, KT - 1, :].bitcast(F32), ALU.subtract).then_inc(c_lo_done, 1)
                split_lo(b)
                if b == 2:
                    dve.wait_ge(consts_set, 4)
                    dve.wait_ge(s_par, 16)
                    dve.wait_ge(s_con, 16)
                    dve.wait_ge(s_row, 16)
                    dve.wait_ge(s_dist, 16)
                    chained(nc.vector.tensor_scalar(small[:, 5, 0:HEADS], row[:, R_SINK:R_SINK + HEADS], -1.0, None,
                                                    ALU.mult))
                if b % 2 and b >= 3 and (b - 3) // 2 < N_PAIRS:
                    evacuate((b - 3) // 2)
                if 30 <= b <= 33:
                    take_scores(2 * (b - 30))
                    take_scores(2 * (b - 30) + 1)
                    if b == 33:
                        sinks()
                if b == 35:
                    denominators()
                    dve.wait_ge(v_turned, 1)
                    for t in range(TT):
                        ins = nc.vector.tensor_copy(v_sb[:, t, :], o_bank[t][:])
                    ins.then_inc(v_copied, 1)
                if 35 <= b < 35 + HEADS:
                    normalize(b - 35)
                if 39 <= b < 39 + HEADS:
                    split_o(b - 39)
                if b < B_CONV:
                    some_taps(TAPS_PER_BLOCK, (b - 3) // 2 + 1 if b >= 3 else 0)
            dve.wait_ge(block_done, N_BLOCKS)
            dve.wait_ge(s_xt, 16)
            layer_norm(0, ln_rows, s_ln1, out_bank, x1_ready)
            for t in range(TT):
                dve.wait_ge(x1_hi_done, t + 1)
                nc.vector.tensor_tensor(x1_lo[:, t, :], xt[:, t, :], x1_hi[:, t, :].bitcast(F32),
                                        ALU.subtract).then_inc(x1_lo_done, 1)

            def per_token(col, n):
                return col.unsqueeze(2).broadcast_to([P, TT, n])

            dve.wait_ge(logits_done, 1)
            chained(nc.vector.tensor_tensor(lg[:], bank[3][:, 0:TT * LOGITS].rearrange("p (t n) -> p t n", t=TT),
                                            row[:, R_BIAS:R_BIAS + LOGITS].unsqueeze(1).broadcast_to([P, TT, LOGITS]),
                                            ALU.add))
            g_log = lg[:, :, 0:GROUPS]
            chained(nc.vector.tensor_reduce(rs[:, 0, :], g_log, X_AXIS, ALU.max))
            nc.vector.tensor_tensor(rg[:, 1, :, :], g_log, per_token(rs[:, 0, :], GROUPS),
                                    ALU.subtract).then_inc(exp_in, 1)
            chained(nc.vector.tensor_tensor(rg[:, 0, :, :], g_log, per_token(rs[:, 0, :], GROUPS), ALU.is_equal))
            chained(nc.vector.tensor_tensor(rg[:, 0, :, :], rg[:, 0, :, :],
                                            rank4.unsqueeze(1).broadcast_to([P, TT, GROUPS]), ALU.mult))
            chained(nc.vector.tensor_reduce(rs[:, 1, :], rg[:, 0, :, :], X_AXIS, ALU.max))
            chained(nc.vector.tensor_tensor(rg[:, 3, :, :], rg[:, 0, :, :], per_token(rs[:, 1, :], GROUPS),
                                            ALU.is_equal))
            nc.vector.tensor_scalar(rg[:, 0, :, :], rg[:, 3, :, :], NEVER, -NEVER, ALU.mult, ALU.add)
            e_log = lg[:, :, GROUPS:].rearrange("p t (g e) -> p t g e", g=GROUPS)

            def by_group(a):
                return a.unsqueeze(3).broadcast_to([P, TT, GROUPS, PER_GROUP])

            def grouped(a):
                return a.rearrange("p t (g e) -> p t g e", g=GROUPS)

            chained(nc.vector.tensor_tensor(grouped(rt[:, 0, :, :]), e_log, by_group(rg[:, 3, :, :]), ALU.mult))
            chained(nc.vector.tensor_tensor(grouped(rt[:, 1, :, :]), grouped(rt[:, 0, :, :]),
                                            by_group(rg[:, 0, :, :]), ALU.add))

            def first_of_largest(logit, one_hot, largest, key):
                chained(nc.vector.tensor_reduce(largest, logit, X_AXIS, ALU.max))
                chained(nc.vector.tensor_tensor(rt[:, 7, :, :], logit, per_token(largest, EXPERTS), ALU.is_equal))
                chained(nc.vector.tensor_tensor(rt[:, 7, :, :], rt[:, 7, :, :],
                                                rank32.unsqueeze(1).broadcast_to([P, TT, EXPERTS]), ALU.mult))
                chained(nc.vector.tensor_reduce(key, rt[:, 7, :, :], X_AXIS, ALU.max))
                chained(nc.vector.tensor_tensor(one_hot, rt[:, 7, :, :], per_token(key, EXPERTS), ALU.is_equal))

            first_of_largest(rt[:, 1, :, :], rt[:, 2, :, :], rs[:, 2, :], rs[:, 3, :])
            chained(nc.vector.scalar_tensor_tensor(rt[:, 3, :, :], rt[:, 2, :, :], -2 * NEVER, rt[:, 1, :, :],
                                                   ALU.mult, ALU.add))
            first_of_largest(rt[:, 3, :, :], rt[:, 4, :, :], rs[:, 4, :], rs[:, 5, :])
            nc.vector.tensor_tensor(rs[:, 7, :], rs[:, 4, :], rs[:, 2, :], ALU.subtract).then_inc(exp_in, 1)
            nc.vector.tensor_tensor(rt[:, 5, :, :], rt[:, 2, :, :], rt[:, 4, :, :], ALU.add).then_inc(onehot_done, 1)
            dve.wait_ge(router_exp, 2)
            nc.vector.tensor_copy(rt[:, 8, :, :], rt[:, 2, :, :])
            chained(nc.vector.tensor_reduce(rs[:, 6, :], rg[:, 2, :, :], X_AXIS, ALU.add))
            chained(nc.vector.tensor_scalar(rs[:, 9, :], rs[:, 8, :], 1.0, None, ALU.add))
            chained(nc.vector.tensor_tensor(rs[:, 10, :], rs[:, 9, :], rs[:, 6, :], ALU.mult))
            chained(nc.vector.reciprocal(rs[:, 11, :], rs[:, 10, :]))
            chained(nc.vector.tensor_tensor(rs[:, 12, :], rs[:, 11, :], rs[:, 8, :], ALU.mult))
            nc.vector.tensor_tensor(rt[:, 2, :, :], rt[:, 2, :, :], per_token(rs[:, 11, :], EXPERTS), ALU.mult)
            dve.wait_ge(onehot_done, 1)
            chained(nc.vector.tensor_tensor(rt[:, 7, :, :], rt[:, 4, :, :], per_token(rs[:, 12, :], EXPERTS),
                                            ALU.mult))
            chained(nc.vector.tensor_tensor(rt[:, 6, :, :], rt[:, 2, :, :], rt[:, 7, :, :], ALU.add))
            dve.wait_ge(ranks_done, 1)
            rank = bank[4][:, 0:TT * EXPERTS].rearrange("p (t n) -> p t n", t=TT)
            nc.vector.scalar_tensor_tensor(rt[:, 0, :, :], rank, 1.0, rt[:, 5, :, :], ALU.add, ALU.mult)
            place = rt[:, 0, :, :]
            chained(nc.vector.tensor_copy(rt[:, 9, 0, :], bank[5][:, 0:EXPERTS]))
            chained(nc.vector.tensor_tensor_scan(rt[:, 9, 1, :], ones[:, 0:EXPERTS], rt[:, 9, 0, :], 0.0,
                                                 ALU.mult, ALU.add))
            chained(nc.vector.tensor_tensor(rt[:, 9, 1, :], rt[:, 9, 1, :], rt[:, 9, 0, :], ALU.subtract))
            chained(nc.vector.scalar_tensor_tensor(rt[:, 3, :, :], rank, 1.0,
                                                   rt[:, 9, 1, :].unsqueeze(1).broadcast_to([P, TT, EXPERTS]),
                                                   ALU.add, ALU.add))
            for n, one_hot in enumerate((rt[:, 8, :, :], rt[:, 4, :, :])):
                chained(nc.vector.tensor_tensor(rt[:, 1, :, :], rt[:, 3, :, :], one_hot, ALU.mult))
                chained(nc.vector.tensor_reduce(rs[:, 13 + n, :], rt[:, 1, :, :], X_AXIS, ALU.add))
            for t in range(TT):
                nc.vector.tensor_scalar(cmp_f[:, t, :], iota, rs[:, 13, t:t + 1], None, ALU.is_equal)
            for t in range(TT):
                if t == 0:
                    chained(nc.vector.tensor_reduce(load_f[:], rt[0:1, 9, 0, :], X_AXIS, ALU.max))
                nc.vector.scalar_tensor_tensor(compact[:, t, :], iota, rs[:, 14, t:t + 1], cmp_f[:, t, :],
                                               ALU.is_equal, ALU.add).then_inc(compact_built, 1)
            for w in range(WINDOWS + 1):
                nc.vector.tensor_scalar(starts_f[:, w, :], rt[0:1, 9, 1, :], float(WIN * w), float(ROUTED),
                                        ALU.add, ALU.min)
            nc.vector.tensor_copy(load_i[:], load_f[:])
            for u in range(2):
                ins = nc.vector.tensor_copy(info[u][:, :, 0:1], con[:, C_TOKEN:C_TOKEN + TT].unsqueeze(2))
            chained(ins)
            nc.vector.tensor_copy(starts[:], starts_f[:]).then_inc(load_known, 1)

            def build_gather(p, u):
                if from_pair(p, 2):
                    dve.wait_ge(info_done, p - 1)
                two = bass.ds(p * 2, 2)
                nc.vector.tensor_tensor(
                    gat[u].rearrange("p t (j s) -> p t j s", j=2),
                    iota[:, 0:WIN].unsqueeze(1).unsqueeze(1).broadcast_to([P, TT, 2, WIN]),
                    place[:, :, two].unsqueeze(3).broadcast_to([P, TT, 2, WIN]), ALU.is_equal)
                nc.vector.tensor_copy(info[u][:, :, 1:3], rt[:, 6, :, two]).then_inc(gat_built, 1)

            def build_more(e, n, u):
                dve.wait_ge(info_done, n - 1)
                nc.vector.memset(sig[:, 0, 0:1], 0.0)
                for j in range(2):
                    nc.vector.tensor_copy(info[u][:, :, 1 + j:2 + j], rt[:, 6, :, bass.ds(e, 1)])
                    ins = nc.vector.tensor_copy(more_place[:, :, j:j + 1], place[:, :, bass.ds(e, 1)])
                ins.then_inc(more_copied, 1)
                dve.wait_ge(more_copied, e * 2 + (u + 1))
                for j in range(2):
                    ins = nc.vector.scalar_tensor_tensor(
                        gat[u][:, :, j * WIN:(j + 1) * WIN],
                        iota[:, 0:WIN].unsqueeze(1).broadcast_to([P, TT, WIN]), float(WIN * (1 + 2 * u + j)),
                        more_place[:, :, j:j + 1].broadcast_to([P, TT, WIN]), ALU.add, ALU.is_equal)
                ins.then_inc(gat_built, 1)

            def gate_times_up(p, u):
                dve.wait_ge(swish_done, p + 1)
                dve.wait_ge(info_copied, p + 1)
                if from_pair(p, 1):
                    dve.wait_ge(h_turned, p)
                nc.vector.scalar_tensor_tensor(h_sb, swished, weight[u], gu_bank[:, HIDDEN:], ALU.mult,
                                               ALU.mult).then_inc(h_ready, 1)

            def build_scatter(p, u):
                if from_pair(p, 2):
                    dve.wait_ge(scattered, p - 1)
                nc.vector.tensor_scalar(sca[u], iota[:, 0:SEQ], token[u], None, ALU.is_equal).then_inc(sca_built, 1)

            def split_y_lo(p):
                for c in range(2):
                    n = slice(c * HALF, (c + 1) * HALF)
                    dve.wait_ge(y_hi_done, 2 * p + (c + 1))
                    nc.vector.tensor_tensor(y_lo[:, n], y_bank[c][:], y_hi[:, n].bitcast(F32),
                                            ALU.subtract).then_inc(y_lo_done, 1)

            def pair(p, u, build=True):
                gate_times_up(p, u)
                build_scatter(p, u)
                if build:
                    build_gather(p + 2, u)
                split_y_lo(p)

            build_gather(0, 0)
            build_gather(1, 1)
            for k in range(1, KT, 2):
                dve.wait_ge(gathered, k + 1)
                nc.vector.tensor_copy(xgT[:, k, 0:ROUTED], free_bank[k % 4][:]).then_inc(xgT_odd, 1)
            for p in range(2):
                pair(p, p)
            with dve.Fori(1, PAIRS // 2 - 1) as i:
                for u in range(2):
                    pair(i * 2 + u, u)
            for p in range(PAIRS - 2, PAIRS):
                pair(p, p % 2, build=False)
            load = dve.value_load(load_i[0:1, 0:1], min_val=0, max_val=SEQ)
            with dve.If(load > WIN):
                with dve.Fori(0, EXPERTS) as e:
                    for u in range(2):
                        n = e * 2 + (PAIRS + u)
                        build_more(e, n, u)
                        gate_times_up(n, u)
                        build_scatter(n, u)
                        split_y_lo(n)
                dve.wait_ge(scattered, PAIRS + 2 * EXPERTS)

            dve.wait_ge(scattered, PAIRS)
            dve.wait_ge(s_ln2, 16)
            layer_norm(1, ln2_rows, s_ln2, moe_bank, result)

        @block.tensor
        def _(pe):
            mm = nc.tensor.matmul

            def three_products(dst, pairs, first, last):
                (ah, al), (bh, bl) = pairs
                mm(dst, ah, bh, start=first, stop=False)
                mm(dst, ah, bl, start=False, stop=False)
                return mm(dst, al, bh, start=False, stop=last)

            def column_block(b, hi, lo, tile_ready=None):
                q = b // 2
                dst = pair_bank[q % PSUM_PAIRS][:, (b % 2) * SEQ:(b % 2 + 1) * SEQ]
                if b % 2 == 0 and q >= PSUM_PAIRS:
                    wait_pair_read(pe, q - PSUM_PAIRS)
                pe.wait_ge(w_lo_done, b + 1)
                for k in range(KT):
                    if tile_ready is not None:
                        pe.wait_ge(tile_ready, k + 1)
                    w = slice(k * P, (k + 1) * P)
                    ins = three_products(dst, ((w_hi[:, b % SPLIT, w], w_lo[:, b % SPLIT, w]),
                                               (hi[:, k, :], lo[:, k, :])), k == 0, k == KT - 1)
                ins.then_inc(block_done, 1)

            def scores(h):
                if h == 0:
                    pe.wait_ge(qkv_copied, (V_BLOCK - Q_BLOCK) // 2)
                if h >= 2:
                    pe.wait_ge(scores_read, h - 1)
                for t in range(TT):
                    ins = mm(score_bank[h % 2][:, t * SEQ:(t + 1) * SEQ], qT[:, h, t * P:(t + 1) * P],
                             kT[:, h // 2, :], start=True, stop=True)
                ins.then_inc(scores_done, 1)

            def turn_v():
                pe.wait_ge(qkv_copied, (GATE_BLOCK - Q_BLOCK) // 2)
                for t in range(TT):
                    for j in range(KV_HEADS):
                        ins = nc.tensor.transpose(o_bank[t][:, j * P:(j + 1) * P], vT[:, j, t * P:(t + 1) * P], ident)
                ins.then_inc(v_turned, 1)

            def turn_p(h):
                pe.wait_ge(prob_ready, h + 1)
                if h >= 1:
                    pe.wait_ge(p_copied, h)
                for kb in range(TT):
                    for t in range(TT):
                        ins = nc.tensor.transpose(t_bank[:, kb * SEQ + t * P:kb * SEQ + (t + 1) * P],
                                                  prob[:, h, t, kb * P:(kb + 1) * P], ident)
                ins.then_inc(p_turned, 1)

            def values(h):
                pe.wait_ge(p_copied, h + 1)
                if h == 0:
                    pe.wait_ge(v_copied, 1)
                if h >= 2:
                    pe.wait_ge(o_lo_done, h - 1)
                for kb in range(TT):
                    ins = mm(o_bank[h % 2][:, 0:SEQ], v_sb[:, kb, (h // 2) * P:(h // 2 + 1) * P],
                             pT[:, h % 2, kb, :], start=(kb == 0), stop=(kb == TT - 1))
                ins.then_inc(pv_done, 1)

            pe.wait_ge(x_lo_done, 1)
            for b in range(N_IN):
                if b == 24:
                    pe.wait_ge(s_con, 16)
                column_block(b, x_hi, x_lo)
                if 29 <= b <= 32:
                    scores(2 * (b - 29))
                    scores(2 * (b - 29) + 1)
                if b == 34:
                    turn_v()
                if 36 <= b < 36 + HEADS:
                    turn_p(b - 36)
                if 37 <= b < 37 + HEADS:
                    values(b - 37)
            for b in range(B_ATTN, B_CONV):
                column_block(b, a_hi, a_lo, o_lo_done if b == B_ATTN else None)
            pe.wait_ge(taps_done, KT * CONV_WIDTH)
            for i in range(KT):
                ins = mm(bank[7][:, 0:SEQ], mean_ones[:], acc[:, i, :], start=(i == 0), stop=(i == KT - 1))
            ins.then_inc(mean_done, 1)
            pe.wait_ge(squared, 1)
            for i in range(KT):
                ins = mm(bank[7][:, SEQ:], mean_ones[:], square[:, i, :], start=(i == 0), stop=(i == KT - 1))
            ins.then_inc(var_done, 1)
            for b in range(B_CONV, B_OUT):
                column_block(b, x_hi, x_lo, c_lo_done if b == B_CONV else None)
            for b in range(B_OUT, N_BLOCKS):
                k = b - B_OUT
                pe.wait_ge(w_lo_done, b + 1)
                pe.wait_ge(m_lo_done, k // 2 + 1)
                for t in range(TT):
                    for c in range(2):
                        n = slice(c * HALF, (c + 1) * HALF)
                        m = slice(t * P, (t + 1) * P)
                        ins = three_products(out_bank[2 * t + c][:], ((a_hi[:, k, m], a_lo[:, k, m]),
                                             (w_hi[:, b % SPLIT, n], w_lo[:, b % SPLIT, n])), k == 0, k == KT - 1)
                ins.then_inc(block_done, 1)

            for t in range(TT):
                pe.wait_ge(x1_ready, t + 1)
                for c in range(2):
                    dst = (pair_bank + [bank[7]])[2 * t + c]
                    for i in range(4):
                        ins = nc.tensor.transpose(dst[:, i * P:(i + 1) * P],
                                                  xt[:, t, (4 * c + i) * P:(4 * c + i + 1) * P], ident)
                    ins.then_inc(x1_turned, 1)
                pe.wait_ge(s_wr, 16)
                pe.wait_ge(x1T_copied, 2 * t + 2)
                for k in range(KT):
                    ins = mm(bank[3][:, t * LOGITS:(t + 1) * LOGITS], x1T[:, k, t * P:(t + 1) * P], wr[:, k, :],
                             start=(k == 0), stop=(k == KT - 1))
            ins.then_inc(logits_done, 1)
            one_hot = rt[:, 5, :, :]
            pe.wait_ge(onehot_done, 1)
            mm(bank[4][:, 0:EXPERTS], tri, one_hot[:, 0, :], start=True, stop=True)
            mm(bank[4][:, EXPERTS:2 * EXPERTS], ones[:], one_hot[:, 0, :], start=True, stop=False)
            mm(bank[4][:, EXPERTS:2 * EXPERTS], tri, one_hot[:, 1, :], start=False, stop=True)
            mm(bank[5][:, 0:EXPERTS], ones[:], one_hot[:, 0, :], start=True, stop=False)
            mm(bank[5][:, 0:EXPERTS], ones[:], one_hot[:, 1, :], start=False, stop=True).then_inc(ranks_done, 1)

            pe.wait_ge(x1_lo_done, TT)
            pe.wait_ge(compact_built, TT)
            for k in range(KT):
                if k >= 4:
                    pe.wait_ge(xgT_odd if k % 2 else xgT_even, (k - 4) // 2 + 1)
                n = slice(k * P, (k + 1) * P)
                for t in range(TT):
                    mm(free_bank[k % 4][:], x1_hi[:, t, n], compact[:, t, :], start=(t == 0), stop=False)
                    ins = mm(free_bank[k % 4][:], x1_lo[:, t, n], compact[:, t, :], start=False, stop=(t == TT - 1))
                ins.then_inc(gathered, 1)

            def slot_info(p, u):
                pe.wait_ge(gat_built, p + 1)
                if from_pair(p, 1):
                    pe.wait_ge(hT_copied, p)
                for t in range(TT):
                    ins = mm(t7_bank[:, 0:3], gat[u][:, t, :], info[u][:, t, :], start=(t == 0), stop=(t == TT - 1))
                ins.then_inc(info_done, 1)

            def gate_up(p, u, slot):
                pe.wait_ge(xg_ready, p + 1)
                if from_pair(p, 1):
                    pe.wait_ge(h_ready, p)
                for k in range(KT):
                    for j in range(2):
                        w = slots[:, slot[j], 0:GU_N].rearrange("p (k n) -> p k n", k=KT)
                        ins = mm(gu_bank[j * WIN:(j + 1) * WIN, :], xg[u][:, k, j * WIN:(j + 1) * WIN],
                                 w[:, k, :], start=(k == 0), stop=(k == KT - 1))
                ins.then_inc(gu_done, 1)

            def turn_h(p):
                pe.wait_ge(h_ready, p + 1)
                pe.wait_ge(info_copied, p + 1)
                for k in range(HT):
                    ins = nc.tensor.transpose(t7_bank[:, k * P:(k + 1) * P], h_sb[:, k * P:(k + 1) * P], ident)
                ins.then_inc(h_turned, 1)

            def down(p, slot):
                pe.wait_ge(hT_copied, p + 1)
                if from_pair(p, 1):
                    pe.wait_ge(y_lo_done, 2 * p)
                for c in range(2):
                    for k in range(HT):
                        for j in range(2):
                            w = slots[:, slot[j], GU_N:SLOT_N].rearrange("p (k n) -> p k n", k=HT)
                            ins = mm(y_bank[c][j * WIN:(j + 1) * WIN, :], hT[:, k, j * WIN:(j + 1) * WIN],
                                     w[:, k, c * HALF:(c + 1) * HALF], start=(k == 0), stop=(k == HT - 1))
                    ins.then_inc(down_done, 1)

            def scatter(p, u, first=False):
                pe.wait_ge(y_lo_done, 2 * p + 2)
                pe.wait_ge(sca_built, p + 1)
                for t in range(TT):
                    for c in range(2):
                        dst = moe_bank[2 * t + c][:]
                        s = sca[u][:, t * P:(t + 1) * P]
                        n = slice(c * HALF, (c + 1) * HALF)
                        mm(dst, s, y_hi[:, n], start=first, stop=False, skip_group_check=True)
                        ins = mm(dst, s, y_lo[:, n], start=False, stop=True, skip_group_check=True)
                ins.then_inc(scattered, 1)

            def pair(p, u, turn, last=False):
                for j in range(2):
                    pe.wait_ge(gu_loaded[2 * u + j], 16 * turn)
                gate_up(p, u, (2 * u, 2 * u + 1))
                if from_pair(p, 1):
                    scatter(p - 1, 1 - u, first=(isinstance(p, int) and p == 1))
                turn_h(p)
                for j in range(2):
                    pe.wait_ge(wd_loaded[2 * u + j], 16 * turn)
                down(p, (2 * u, 2 * u + 1))
                if not last:
                    slot_info(p + 1, 1 - u)

            pe.wait_ge(xgT_odd, KT // 2)
            pe.wait_ge(xgT_even, KT // 2)
            slot_info(0, 0)
            for p in range(2):
                pair(p, p, 1)
            with pe.Fori(1, PAIRS // 2 - 1) as i:
                for u in range(2):
                    pair(i * 2 + u, u, i + 1)
            for p in range(PAIRS - 2, PAIRS):
                pair(p, p % 2, PAIRS // 2, last=(p == PAIRS - 1))
            scatter(PAIRS - 1, 1)

            load = pe.value_load(load_i[0:1, 0:1], min_val=0, max_val=SEQ)
            with pe.If(load > WIN):
                with pe.Fori(0, EXPERTS) as e:
                    pe.wait_ge(more_loaded, e * 32 + 32)
                    for u in range(2):
                        n = e * 2 + (PAIRS + u)
                        slot_info(n, u)
                        gate_up(n, u, (0, 0))
                        turn_h(n)
                        down(n, (0, 0))
                        scatter(n, u)


def kernel(x, w_in, b_gate, w_dw, b_dw, conv_ln_g, conv_ln_b, w_conv_proj, attn_sink, w_attn_proj, w_out,
           ln1_g, ln1_b, w_router_group, b_router_group, w_router_expert, b_router_expert, w_gate_up, w_down,
           ln2_g, ln2_b):
    import concourse.bacc as bacc
    from concourse.bass_utils import run_bass_kernel_spmd

    def blocks(w, n):
        return w.reshape(KT, P, n, P).transpose(2, 1, 0, 3).reshape(n, P, KT * P)

    def channels(v):
        return v.reshape(KT, P, -1).transpose(1, 0, 2).reshape(P, -1)

    given = {k: np.asarray(v) for k, v in dict(
        x=x, w_in=w_in, b_gate=b_gate, w_dw=w_dw, b_dw=b_dw, g=conv_ln_g, b=conv_ln_b, w_conv=w_conv_proj,
        sink=attn_sink, w_attn=w_attn_proj, w_out=w_out, ln1_g=ln1_g, ln1_b=ln1_b, rg=w_router_group,
        brg=b_router_group, re=w_router_expert, bre=b_router_expert, gu=w_gate_up, wd=w_down, ln2_g=ln2_g,
        ln2_b=ln2_b).items()}
    g = {k: v[0] for k, v in given.items()}
    arrays = {
        "xT": g["x"].T.reshape(KT, P, SEQ).transpose(1, 0, 2),
        "x": g["x"],
        "consts": constants(),
        "dists": distances(),
        "chan": np.concatenate([g["b_gate"].reshape(2 * KT, P).T, channels(g["w_dw"].T), channels(g["b_dw"]),
                                channels(g["g"]), channels(g["b"])], axis=1),
        "rows": np.concatenate([g["brg"], g["bre"], g["sink"]])[None, :],
        "w_in": blocks(g["w_in"], N_IN),
        "w_attn": blocks(g["w_attn"], KT),
        "w_conv": blocks(g["w_conv"], KT),
        "w_out": g["w_out"],
        "ln1": np.stack([g["ln1_g"], g["ln1_b"]])[None],
        "ln2": np.stack([g["ln2_g"], g["ln2_b"]])[None],
        "w_router": np.concatenate([g["rg"], g["re"]], axis=1).reshape(KT, P, LOGITS).transpose(1, 0, 2),
        "w_gate_up": g["gu"].reshape(EXPERTS, KT, P, 2 * HIDDEN).transpose(0, 2, 1, 3).reshape(EXPERTS, P, GU_N),
        "w_down": g["wd"].reshape(EXPERTS, HT, P, D).transpose(0, 2, 1, 3).reshape(EXPERTS, P, WD_N),
    }
    nc = bacc.Bacc("TRN2", target_bir_lowering=False, num_devices=1)
    sent, args = {}, []
    for name, a in arrays.items():
        sent[f"in_{name}"] = np.ascontiguousarray(a)
        args.append(nc.dram_tensor(f"in_{name}", a.shape, F32, kind="ExternalInput").ap())
    out = nc.dram_tensor("out_x", (SEQ, D), F32, kind="ExternalOutput").ap()
    encoder_kernel(nc, *args, out)
    result = run_bass_kernel_spmd(nc, [sent], core_ids=[0])
    return result.results[0]["out_x"].reshape(1, SEQ, D)
```

```python
from contextlib import ExitStack

import concourse.bass as bass
import numpy as np
from concourse import mybir

F32 = mybir.dt.float32
F32R = mybir.dt.float32r
I32 = mybir.dt.int32
ALU = mybir.AluOpType
ACT = mybir.ActivationFunctionType
X_AXIS = mybir.AxisListType.X

P = 128
D = 1024
SEQ = 256
HEADS, KV_HEADS = 8, 4
CONV_WIDTH = 31
PAD = (CONV_WIDTH - 1) // 2
WINDOW = 128
GROUPS, PER_GROUP = 4, 8
EXPERTS = GROUPS * PER_GROUP
HIDDEN = D // 4
LN_EPS = 1e-5
ALPHA = 2.0 ** 0.25
SCALE = float(P) ** -0.5
FAR = 3e32
NEVER = 1e30

KT = D // P
TT = SEQ // P
HT = HIDDEN // P
LOGITS = GROUPS + EXPERTS
HALF = 512

ORDER = [c for i in range(KT) for c in (i, KT + i)]
ORDER += list(range(16, 32)) + list(range(40, 48)) + list(range(32, 40))
N_IN = len(ORDER)
B_ATTN, B_CONV, B_OUT = N_IN, N_IN + KT, N_IN + 2 * KT
N_BLOCKS = N_IN + 3 * KT
VAR_PAIR = B_CONV // 2
Q_BLOCK, V_BLOCK, GATE_BLOCK = 16, 28, 32

RAW = 4
SPLIT = 2
PSUM_PAIRS = 3
DVE_TAPS = KT * (CONV_WIDTH - 1)
TAPS_PER_BLOCK = 5
NATIVE = (0, 1) + tuple(range(9, 40, 2))


def split_block(n):
    return [b for b in range(N_BLOCKS) if b not in NATIVE][n]


def splits_before(b):
    return b - sum(n < b for n in NATIVE)


WIN = 64
PAIRS = EXPERTS // 2
WINDOWS = SEQ // WIN
ROUTED = 2 * SEQ
SLOTS = 4
GU_N = KT * 2 * HIDDEN
GU_HALF = GU_N // 2
WD_N = HT * D
SLOT_N = GU_N + WD_N

C_IDENT, C_TRI, C_IOTA = 0, P, 2 * P
C_RANK4 = C_IOTA + ROUTED
C_RANK32 = C_RANK4 + GROUPS
C_TOKEN = C_RANK32 + EXPERTS
C_END = C_TOKEN + TT
A_BGATE = 0
A_WDW = 16
A_BDW = A_WDW + KT * CONV_WIDTH
A_LNG = A_BDW + KT
A_LNB = A_LNG + KT
A_END = A_LNB + KT
R_BIAS, R_SINK, R_END = 0, LOGITS, LOGITS + HEADS


def constants():
    c = np.zeros((P, C_END), np.float32)
    c[:, C_IDENT:C_IDENT + P] = np.eye(P)
    c[:, C_TRI:C_TRI + P] = np.arange(P)[:, None] < np.arange(P)[None, :]
    c[:, C_IOTA:C_IOTA + ROUTED] = np.arange(1, ROUTED + 1)
    c[:, C_RANK4:C_RANK4 + GROUPS] = np.arange(GROUPS, 0, -1)
    c[:, C_RANK32:C_RANK32 + EXPERTS] = np.arange(EXPERTS, 0, -1)
    c[:, C_TOKEN:C_TOKEN + TT] = 1 + np.arange(P)[:, None] + P * np.arange(TT)[None, :]
    return c


def distances():
    q = np.arange(P)[:, None, None] + P * np.arange(TT)[None, :, None]
    dist = np.abs(q - np.arange(SEQ)[None, None, :]).astype(np.float32)
    return np.where(dist <= WINDOW, dist, np.float32(FAR)).reshape(P, TT * SEQ)


def encoder_kernel(nc, xT, x, consts, dists, chan, rows, w_in, w_attn, w_conv, w_out, ln1, ln2, w_router,
                   w_gate_up, w_down, out):
    with ExitStack() as ctx:
        def sb(name, shape, dt=F32):
            return ctx.enter_context(nc.sbuf_tensor(name, shape, dt))

        def sem(name):
            return ctx.enter_context(nc.semaphore(name))

        slots = sb("slots", [P, SLOTS, SLOT_N])
        con = sb("con", [P, C_END])
        par = sb("par", [P, A_END])
        row = sb("row", [P, R_END])
        xt = sb("xt", [P, TT, D])
        raw = sb("raw", [P, RAW, D])
        gates = sb("gates", [P, 18, SEQ])
        kT = sb("kT", [P, KV_HEADS, SEQ])
        pT = sb("pT", [P, 2, TT, SEQ])
        sig = sb("sig", [P, 2, SEQ])
        wr = sb("wr", [P, KT, LOGITS])
        x_hi, x_lo = sb("x_hi", [P, KT, SEQ], F32R), sb("x_lo", [P, KT, SEQ], F32R)
        a_at = nc.sbuf_base
        a_hi, a_lo = sb("a_hi", [P, KT, SEQ], F32R), sb("a_lo", [P, KT, SEQ], F32R)
        w_hi, w_lo = sb("w_hi", [P, SPLIT, D], F32R), sb("w_lo", [P, SPLIT, D], F32R)
        ones = sb("ones", [P, P])
        mean_ones = sb("mean_ones", [P, P])
        alpha_ident = sb("alpha_ident", [P, P])
        eps = sb("eps", [P, 1])
        small = sb("small", [P, 8, 2 * HEADS])
        stat = sb("stat", [P, TT, 2, 6])
        mv = sb("mv", [P, TT, 4])
        rt = sb("rt", [P, 10, TT, EXPERTS])
        rs = sb("rs", [P, 16, TT])
        rg = sb("rg", [P, 4, TT, GROUPS])
        lg = sb("lg", [P, TT, LOGITS])
        load_f = sb("load_f", [1, 1])
        load_i = sb("load_i", [1, 1], I32)
        starts_f = raw[0:1, 3, 0:(WINDOWS + 1) * EXPERTS].rearrange("p (w e) -> p w e", e=EXPERTS)
        starts = sb("starts", [1, WINDOWS + 1, EXPERTS], I32)

        over = slots[:, 2:4, :].rearrange("p s n -> p (s n)")
        at = [0]

        def carve(n):
            at[0] += n
            return over[:, at[0] - n:at[0]]

        h_pad = carve(KT * (SEQ + 2 * PAD)).rearrange("p (i t) -> p i t", i=KT)
        acc = carve(KT * SEQ).rearrange("p (i t) -> p i t", i=KT)
        qT = carve(HEADS * SEQ).rearrange("p (i t) -> p i t", i=HEADS)
        v_sb = carve(TT * KV_HEADS * P).rearrange("p (t n) -> p t n", t=TT)
        prob = carve(HEADS * TT * SEQ).rearrange("p (h t n) -> p h t n", h=HEADS, t=TT)
        dist = carve(TT * SEQ)
        assert at[0] <= 2 * SLOT_N
        square = h_pad.rearrange("p i t -> p (i t)")[:, 0:KT * SEQ].rearrange("p (i t) -> p i t", i=KT)
        xT_raw = gates[:, 0:KT, :]
        ln_rows = gates[:, 0:8, :].rearrange("p (a b) t -> p a (b t)", a=2)
        vT = gates[:, 12:16, :]
        ln2_rows = raw[:, 2:4, :]
        x1T = raw[:, 0:2, :].rearrange("p a (b t) -> p (a b) t", t=SEQ)

        x1_hi = x_hi[:].rearrange("p i t -> p (i t)").rearrange("p (t n) -> p t n", t=TT)
        x1_lo = x_lo[:].rearrange("p i t -> p (i t)").rearrange("p (t n) -> p t n", t=TT)
        compact = w_hi[:, 1, :].rearrange("p (t n) -> p t n", t=TT)
        xgT = gates[:].rearrange("p a t -> p (a t)").rearrange("p (k n) -> p k n", k=KT)
        y_hi, y_lo = w_hi[:, 0, :], w_lo[:, 0, :]
        first_places = w_hi[:, 0, 0:2 * SEQ].rearrange("p (t n) -> p t n", t=TT)
        spare_sb = nc.alloc_sbuf_tensor_at("spare", [P, 2, GU_HALF], F32, offset=a_at)
        spare = [spare_sb[:, c, :] for c in range(2)]
        scatter_matrix = [w_lo[:, 1, SEQ * i:SEQ * (i + 1)] for i in range(2)]
        xg = [raw[:, i, :].rearrange("p (k n) -> p k n", k=KT) for i in range(2)]
        first_xg = raw[:, 0:2, :].rearrange("p u (k n) -> p k u n", k=KT)
        gat = [pT[:, 0, i, :].rearrange("p (t n) -> p t n", t=TT) for i in range(2)]
        swished, h_sb = pT[:, 1, 0, :], pT[:, 1, 1, :]
        hT = kT[:, 0, :].rearrange("p (k n) -> p k n", k=HT)
        info = [kT[:, 1, 16 * i:16 * i + 3 * TT].rearrange("p (t c) -> p t c", t=TT) for i in range(2)]
        token = [kT[:, 1, 32 + i:33 + i] for i in range(2)]
        weight = [kT[:, 1, 34 + i:35 + i] for i in range(2)]
        more_place = kT[:, 1, 40:40 + 2 * TT].rearrange("p (t j) -> p t j", t=TT)

        ident = con[:, C_IDENT:C_IDENT + P]
        tri = con[:, C_TRI:C_TRI + P]
        iota = con[:, C_IOTA:C_IOTA + ROUTED]
        rank4 = con[:, C_RANK4:C_RANK4 + GROUPS]
        rank32 = con[:, C_RANK32:C_RANK32 + EXPERTS]

        bank = [ctx.enter_context(nc.psum_tensor(f"bank{i}", [P, HALF], F32)) for i in range(8)]
        pair_bank = bank[0:3]
        score_bank = bank[3:5]
        t_bank, o_bank = bank[5], [bank[6], bank[7]]
        var_bank = pair_bank[VAR_PAIR % PSUM_PAIRS]
        out_bank = [bank[3], bank[4], bank[5], bank[6]]
        first_choice = raw[:, 2, :].rearrange("p (t n) -> p t n", t=TT)
        first_bank = [bank[1], bank[2], bank[3], bank[6]]
        gu_bank, y_bank, turn_bank = bank[0], [bank[1], bank[2]], bank[7]

        s_xT = [sem(f"s_xT{c}") for c in range(2)]
        s_con, s_par, s_row, s_xt = (sem(n) for n in ("s_con", "s_par", "s_row", "s_xt"))
        s_ln1, s_ln2, s_wr, s_out = (sem(n) for n in ("s_ln1", "s_ln2", "s_wr", "s_out"))
        raw_loaded = [sem(f"raw_loaded{i}") for i in range(RAW)]
        gu_loaded = [[sem(f"gu_loaded{i}_{c}") for c in range(2)] for i in range(SLOTS)]
        spare_loaded = [sem(f"spare_loaded{c}") for c in range(2)]
        wd_loaded = [sem(f"wd_loaded{i}") for i in range(SLOTS)]
        consts_set, alpha_set = sem("consts_set"), sem("alpha_set")
        x_hi_done, x_lo_done = sem("x_hi_done"), sem("x_lo_done")
        w_hi_done, w_lo_done = sem("w_hi_done"), sem("w_lo_done")
        block_done = sem("block_done")
        sigmoid_done, glu_done = sem("sigmoid_done"), sem("glu_done")
        qkv_copied, gates_done = sem("qkv_copied"), sem("gates_done")
        first_tap_done, taps_done = sem("first_tap_done"), sem("taps_done")
        denominators_done = sem("denominators_done")
        scores_done, scores_read = sem("scores_done"), sem("scores_read")
        neg_max_done, exp_done, sink_in, sink_exp = (
            sem(n) for n in ("neg_max_done", "exp_done", "sink_in", "sink_exp"))
        v_turned, v_copied = sem("v_turned"), sem("v_copied")
        prob_ready, p_turned, p_copied = sem("prob_ready"), sem("p_turned"), sem("p_copied")
        pv_done, o_hi_done, o_lo_done = sem("pv_done"), sem("o_hi_done"), sem("o_lo_done")
        attn_gated, conv_gated, merged = sem("attn_gated"), sem("conv_gated"), sem("merged")
        m_hi_done, m_lo_done = sem("m_hi_done"), sem("m_lo_done")
        mean_done, centered, squared, var_done = (sem(n) for n in ("mean_done", "centered", "squared", "var_done"))
        std_done, scaled, silu_done, c_hi_done, c_lo_done = (
            sem(n) for n in ("std_done", "scaled", "silu_done", "c_hi_done", "c_lo_done"))
        dve_step = sem("dve_step")
        ln_var, ln_std, x1_ready, x1_hi_done, x1_lo_done = (
            sem(n) for n in ("ln_var", "ln_std", "x1_ready", "x1_hi_done", "x1_lo_done"))
        x1_turned, x1T_copied, logits_done = sem("x1_turned"), sem("x1T_copied"), sem("logits_done")
        exp_in, router_exp, onehot_done, ranks_done, load_known = (
            sem(n) for n in ("exp_in", "router_exp", "onehot_done", "ranks_done", "load_known"))
        s_dist = sem("s_dist")
        first_built, first_gathered, first_copied = (
            sem(n) for n in ("first_built", "first_gathered", "first_copied"))
        compact_built, gathered, xgT_even, xgT_odd, pads_set = (
            sem(n) for n in ("compact_built", "gathered", "xgT_even", "xgT_odd", "pads_set"))
        xg_ready, gat_built, info_done, info_copied, scatter_built = (
            sem(n) for n in ("xg_ready", "gat_built", "info_done", "info_copied", "scatter_built"))
        gu_done, swish_done, h_ready, h_turned, hT_copied = (
            sem(n) for n in ("gu_done", "swish_done", "h_ready", "h_turned", "hT_copied"))
        down_done, y_hi_done, y_lo_done, scattered = (
            sem(n) for n in ("down_done", "y_hi_done", "y_lo_done", "scattered"))
        more_loaded, more_copied = sem("more_loaded"), sem("more_copied")
        result = sem("result")

        def from_pair(p, n):
            return not isinstance(p, int) or p >= n

        def is_pair(p, n):
            return isinstance(p, int) and p == n

        def block_of(b):
            if b < B_ATTN:
                return w_in[ORDER[b]]
            if b < B_CONV:
                return w_attn[b - B_ATTN]
            if b < B_OUT:
                return w_conv[b - B_CONV]
            return w_out[(b - B_OUT) * P:(b - B_OUT + 1) * P, :]

        def wait_pair_read(eng, q):
            if q < Q_BLOCK // 2:
                eng.wait_ge(glu_done, q + 1)
            elif q < GATE_BLOCK // 2:
                eng.wait_ge(qkv_copied, q - Q_BLOCK // 2 + 1)
            elif q < N_IN // 2:
                eng.wait_ge(gates_done, q - GATE_BLOCK // 2 + 1)
            elif q < B_CONV // 2:
                eng.wait_ge(attn_gated, q - N_IN // 2 + 1)
            else:
                eng.wait_ge(conv_gated, q - B_CONV // 2 + 1)

        block = ctx.enter_context(nc.Block())

        @block.sync
        def _(sp):
            def load_gate_up(e, s):
                for c in range(2):
                    n = slice(c * GU_HALF, (c + 1) * GU_HALF)
                    sp.dma_start(slots[:, s, n], w_gate_up[e, :, n]).then_inc(gu_loaded[s][c], 16)

            def load_down(e):
                sp.dma_start(slots[:, e % SLOTS, GU_N:SLOT_N], w_down[e]).then_inc(wd_loaded[e % SLOTS], 16)

            for c in range(2):
                sp.dma_start(xT_raw[:, 4 * c:4 * c + 4, :], xT[:, 4 * c:4 * c + 4, :]).then_inc(s_xT[c], 16)
                sp.dma_start(raw[:, c, :], block_of(c)).then_inc(raw_loaded[c], 16)
            for b in range(2, N_BLOCKS):
                if b >= RAW and b - RAW in NATIVE:
                    sp.wait_ge(block_done, b - RAW + 1)
                elif b >= RAW:
                    sp.wait_ge(w_lo_done, splits_before(b - RAW) + 1)
                sp.dma_start(raw[:, b % RAW, :], block_of(b)).then_inc(raw_loaded[b % RAW], 16)
                if b == 2:
                    sp.dma_start(par[:], chan).then_inc(s_par, 16)
                    sp.dma_start(con[:], consts).then_inc(s_con, 16)
                    sp.dma_start(dist, dists).then_inc(s_dist, 16)
                    sp.dma_start(row[:], rows.broadcast_to([P, R_END])).then_inc(s_row, 16)
                if b == 10:
                    load_gate_up(0, 0)
                if b == 14:
                    load_gate_up(1, 1)
                if b == 18:
                    load_down(0)
                    load_down(1)
                if b == 22:
                    sp.dma_start(xt[:], x.rearrange("(t p) n -> p t n", p=P)).then_inc(s_xt, 16)
                    sp.dma_start(wr[:], w_router).then_inc(s_wr, 16)
            sp.wait_ge(m_lo_done, KT // 2)
            sp.dma_start(ln_rows, ln1.broadcast_to([P, 2, D])).then_inc(s_ln1, 16)
            sp.wait_ge(silu_done, KT)
            sp.wait_ge(pv_done, HEADS)
            for e in (2, 3):
                load_gate_up(e, e)
            for e in (2, 3):
                load_down(e)
            sp.wait_ge(block_done, N_BLOCKS)
            for c in range(2):
                n = slice(c * GU_HALF, (c + 1) * GU_HALF)
                sp.dma_start(spare[c], w_gate_up[SLOTS, :, n]).then_inc(spare_loaded[c], 16)
            sp.wait_ge(load_known, 1)
            sp.dma_start(ln2_rows, ln2.broadcast_to([P, 2, D])).then_inc(s_ln2, 16)
            load = sp.value_load(load_i[0:1, 0:1], min_val=0, max_val=SEQ)

            def refill(i, spared=False):
                for s in range(SLOTS):
                    if s % 2 == 0:
                        sp.wait_ge(gu_done, i * 2 + (s // 2 - 1))
                    if s or not spared:
                        load_gate_up(i * SLOTS + s, s)
                    if s % 2:
                        sp.wait_ge(down_done, i * 4 + (s // 2 * 2 - 2))
                        for r in (s - 1, s):
                            sp.dma_start(slots[:, r, GU_N:SLOT_N], w_down[i * SLOTS + r]).then_inc(wd_loaded[r], 16)

            refill(1, spared=True)
            with sp.Fori(2, EXPERTS // SLOTS) as i:
                refill(i)
            with sp.If(load > WIN):
                with sp.Fori(0, EXPERTS) as e:
                    sp.wait_ge(scattered, e * 2 + PAIRS)
                    sp.dma_start(slots[:, 0, 0:GU_N], w_gate_up[e]).then_inc(more_loaded, 16)
                    sp.dma_start(slots[:, 0, GU_N:SLOT_N], w_down[e]).then_inc(more_loaded, 16)
            for t in range(TT):
                for c in range(2):
                    n = slice(c * HALF, (c + 1) * HALF)
                    sp.wait_ge(result, 2 * t + c + 1)
                    sp.dma_start(out[t * P:(t + 1) * P, n], xt[:, t, n]).then_inc(s_out, 16)
            sp.wait_ge(s_out, 16 * 2 * TT)

        @block.gpsimd
        def _(pool):
            nc.gpsimd.memset(h_pad, 0.0).then_inc(consts_set, 1)
            nc.gpsimd.memset(ones[:], 1.0).then_inc(consts_set, 1)
            nc.gpsimd.memset(mean_ones[:], 1.0 / D).then_inc(consts_set, 1)
            nc.gpsimd.memset(eps[:], LN_EPS).then_inc(consts_set, 1)
            pool.wait_ge(s_con, 16)
            nc.gpsimd.tensor_scalar(alpha_ident[:], ident, ALPHA, None, ALU.mult).then_inc(alpha_set, 1)

            pool.wait_ge(x1_ready, 2 * TT)
            nc.gpsimd.memset(xgT[:, :, ROUTED:], 0.0).then_inc(pads_set, 1)

            def take_tokens(u, first, second):
                for j, w in enumerate((first, second)):
                    at = pool.value_load(starts[0:1, w[0], w[1]], min_val=0, max_val=ROUTED)
                    ins = nc.gpsimd.tensor_copy(xg[u][:, :, j * WIN:(j + 1) * WIN], xgT[:, :, bass.ds(at, WIN)])
                ins.then_inc(xg_ready, 1)

            pool.wait_ge(load_known, 1)
            pool.wait_ge(pads_set, 1)
            pool.wait_ge(xgT_even, KT // 2)
            pool.wait_ge(xgT_odd, KT // 2)
            with pool.Fori(1, PAIRS // 2) as i:
                for u in range(2):
                    pool.wait_ge(gu_done, i * 2 + (u - 1))
                    take_tokens(u, (0, bass.ds(i * 4 + 2 * u, 1)), (0, bass.ds(i * 4 + (2 * u + 1), 1)))
            load = pool.value_load(load_i[0:1, 0:1], min_val=0, max_val=SEQ)
            with pool.If(load > WIN):
                with pool.Fori(0, EXPERTS) as e:
                    for u in range(2):
                        pool.wait_ge(gu_done, e * 2 + (PAIRS + u - 1))
                        take_tokens(u, (1 + 2 * u, bass.ds(e, 1)), (2 + 2 * u, bass.ds(e, 1)))

        @block.scalar
        def _(act):
            def split_hi(b):
                act.wait_ge(raw_loaded[b % RAW], 16 * (b // RAW + 1))
                n = splits_before(b)
                if n >= SPLIT:
                    act.wait_ge(block_done, split_block(n - SPLIT) + 1)
                nc.scalar.copy(w_hi[:, n % SPLIT, :], raw[:, b % RAW, :]).then_inc(w_hi_done, 1)

            def evacuate(q):
                src = pair_bank[q % PSUM_PAIRS]
                act.wait_ge(block_done, 2 * q + 2)
                if q < Q_BLOCK // 2:
                    if q >= 2:
                        act.wait_ge(glu_done, q - 1)
                    nc.scalar.activation(sig[:, q % 2, :], src[:, SEQ:], ACT.Sigmoid).then_inc(sigmoid_done, 1)
                elif q < GATE_BLOCK // 2:
                    n = 2 * (q - Q_BLOCK // 2)
                    dst = qT[:, n:n + 2, :] if n < HEADS else (
                        kT[:, n - 8:n - 6, :] if n < 12 else vT[:, n - 12:n - 10, :])
                    nc.scalar.copy(dst, src[:].rearrange("p (a t) -> p a t", a=2)).then_inc(qkv_copied, 1)
                elif q < N_IN // 2:
                    if q == GATE_BLOCK // 2:
                        act.wait_ge(s_par, 16)
                        act.wait_ge(x_lo_done, 2)
                    if q == GATE_BLOCK // 2 + 2:
                        act.wait_ge(v_turned, 1)
                    for j in range(2):
                        c = ORDER[2 * q + j] - GATE_BLOCK
                        ins = nc.scalar.activation(gates[:, c, :], src[:, j * SEQ:(j + 1) * SEQ], ACT.Sigmoid,
                                                   bias=par[:, A_BGATE + c:A_BGATE + c + 1])
                    ins.then_inc(gates_done, 1)
                elif q >= B_CONV // 2:
                    m = q - B_CONV // 2
                    act.wait_ge(merged, m + 1)
                    nc.scalar.copy(a_hi[:, 2 * m:2 * m + 2, :], gates[:, 2 * m:2 * m + 2, :]).then_inc(m_hi_done, 1)

            def exponentials(h):
                act.wait_ge(neg_max_done, h // 2 + 1)
                for t in range(TT):
                    ins = nc.scalar.activation(prob[:, h, t, :], prob[:, h, t, :], ACT.Exp, scale=SCALE,
                                               bias=small[:, 1, TT * h + t:TT * h + t + 1],
                                               accum_out=small[:, 2, TT * h + t:TT * h + t + 1])
                ins.then_inc(exp_done, 1)

            def normalize(h):
                for t in range(TT):
                    ins = nc.scalar.mul(prob[:, h, t, :], prob[:, h, t, :], small[:, 7, TT * h + t:TT * h + t + 1])
                ins.then_inc(prob_ready, 1)

            def first_tap(i):
                act.wait_ge(glu_done, i + 1)
                nc.scalar.activation(acc[:, i, :], h_pad[:, i, 0:SEQ], ACT.Identity,
                                     scale=par[:, A_WDW + i * CONV_WIDTH:A_WDW + i * CONV_WIDTH + 1],
                                     bias=par[:, A_BDW + i:A_BDW + i + 1]).then_inc(first_tap_done, 1)

            def copy_pT(h):
                act.wait_ge(p_turned, h + 1)
                if h >= 2:
                    act.wait_ge(pv_done, h - 1)
                nc.scalar.copy(pT[:, h % 2, :, :], t_bank[:].rearrange("p (a t) -> p a t", a=2)).then_inc(p_copied, 1)

            def split_o(h):
                act.wait_ge(pv_done, h + 1)
                nc.scalar.copy(a_hi[:, h, :], o_bank[h % 2][:, 0:SEQ]).then_inc(o_hi_done, 1)

            for c in range(2):
                act.wait_ge(s_xT[c], 16)
                nc.scalar.copy(x_hi[:, 4 * c:4 * c + 4, :], xT_raw[:, 4 * c:4 * c + 4, :]).then_inc(x_hi_done, 1)
            for b in range(N_BLOCKS):
                if b == B_CONV:
                    for m in range(0, KT, 2):
                        act.wait_ge(centered, m // 2 + 1)
                        nc.scalar.activation(square[:, m:m + 2, :], acc[:, m:m + 2, :],
                                             ACT.Square).then_inc(squared, 1)
                    split_hi(b)
                    split_hi(b + 1)
                    act.wait_ge(var_done, 1)
                    act.wait_ge(consts_set, 4)
                    nc.scalar.activation(sig[:, 0, :], var_bank[:, 0:SEQ], ACT.Sqrt,
                                         bias=eps[:, 0:1]).then_inc(std_done, 1)
                    nc.scalar.activation(mv[:, 0, 3:4], eps[:, 0:1], ACT.Silu)
                    act.wait_ge(x_lo_done, 2)
                    act.wait_ge(block_done, N_IN)
                    for i in range(KT + 1):
                        if i < KT:
                            act.wait_ge(scaled, i + 1)
                            nc.scalar.activation(acc[:, i, :], acc[:, i, :], ACT.Silu,
                                                 scale=par[:, A_LNG + i:A_LNG + i + 1],
                                                 bias=par[:, A_LNB + i:A_LNB + i + 1]).then_inc(silu_done, 1)
                        if i >= 1:
                            act.wait_ge(silu_done, i)
                            nc.scalar.copy(x_hi[:, i - 1, :], acc[:, i - 1, :]).then_inc(c_hi_done, 1)
                if b not in NATIVE and b not in (B_CONV, B_CONV + 1):
                    split_hi(b)
                if b % 2 and b >= 3:
                    q = (b - 3) // 2
                    if q < B_OUT // 2:
                        evacuate(q)
                if 31 <= b <= 34:
                    for h in (2 * (b - 31), 2 * (b - 31) + 1):
                        exponentials(h)
                    if b == 34:
                        act.wait_ge(sink_in, 1)
                        nc.scalar.activation(small[:, 4, :], small[:, 3, :], ACT.Exp).then_inc(sink_exp, 1)
                if b == 35:
                    act.wait_ge(v_turned, 1)
                    for t in range(TT):
                        ins = nc.scalar.copy(v_sb[:, t, :], o_bank[t][:])
                    ins.then_inc(v_copied, 1)
                    act.wait_ge(denominators_done, 1)
                if 35 <= b < 35 + HEADS:
                    normalize(b - 35)
                if b % 2 and b >= 5 and (b - 5) // 2 < KT:
                    if b == 5:
                        act.wait_ge(consts_set, 4)
                        act.wait_ge(s_par, 16)
                    first_tap((b - 5) // 2)
                if 38 <= b < 38 + HEADS:
                    copy_pT(b - 38)
                if 39 <= b < 39 + HEADS:
                    split_o(b - 39)

            for t in range(TT):
                act.wait_ge(ln_var, t + 1)
                nc.scalar.activation(mv[:, t, 2:3], mv[:, t, 1:2], ACT.Sqrt, bias=eps[:, 0:1]).then_inc(ln_std, 1)
            for t in range(TT):
                act.wait_ge(x1_ready, 2 * t + 2)
                nc.scalar.copy(x1_hi[:, t, :], xt[:, t, :]).then_inc(x1_hi_done, 1)
                for c in range(2):
                    act.wait_ge(x1_turned, 2 * t + c + 1)
                    src = (pair_bank + [bank[7]])[2 * t + c]
                    nc.scalar.copy(x1T[:, 4 * c:4 * c + 4, t * P:(t + 1) * P],
                                   src[:].rearrange("p (a t) -> p a t", a=4)).then_inc(x1T_copied, 1)
            act.wait_ge(exp_in, 1)
            nc.scalar.activation(rg[:, 2, :, :], rg[:, 1, :, :], ACT.Exp).then_inc(router_exp, 1)
            act.wait_ge(exp_in, 2)
            nc.scalar.activation(rs[:, 8, :], rs[:, 7, :], ACT.Exp).then_inc(router_exp, 1)

            def copy_info(p, u):
                act.wait_ge(info_done, p + 1)
                if from_pair(p, 2):
                    act.wait_ge(h_ready, p - 1)
                    act.wait_ge(scatter_built, p - 1)
                nc.scalar.copy(token[u], turn_bank[:, 0:1])
                for j in range(2):
                    ins = nc.scalar.copy(weight[u][j * WIN:(j + 1) * WIN, :],
                                         turn_bank[j * WIN:(j + 1) * WIN, 1 + j:2 + j])
                ins.then_inc(info_copied, 1)

            def swish(p):
                act.wait_ge(gu_done, p + 1)
                if from_pair(p, 1):
                    act.wait_ge(h_ready, p)
                nc.scalar.activation(swished, gu_bank[:, 0:HIDDEN], ACT.Silu).then_inc(swish_done, 1)

            def copy_hT(p):
                act.wait_ge(h_turned, p + 1)
                if from_pair(p, 1):
                    act.wait_ge(down_done, 2 * p)
                nc.scalar.copy(hT, turn_bank[:, 0:HT * P].rearrange("p (k n) -> p k n", k=HT)).then_inc(hT_copied, 1)

            def split_y_hi(p):
                for c in range(2):
                    act.wait_ge(down_done, 2 * p + (c + 1))
                    if c == 0 and from_pair(p, 1):
                        act.wait_ge(scattered, p)
                    nc.scalar.copy(y_hi[:, c * HALF:(c + 1) * HALF], y_bank[c][:]).then_inc(y_hi_done, 1)

            def copy_sorted():
                for k in range(0, KT, 2):
                    act.wait_ge(gathered, k + 1)
                    nc.scalar.copy(xgT[:, k, 0:ROUTED], out_bank[k % 4][:]).then_inc(xgT_even, 1)

            def pair(p, u, last=False):
                swish(p)
                if is_pair(p, 1):
                    copy_sorted()
                copy_hT(p)
                split_y_hi(p)
                if not last:
                    copy_info(p + 1, 1 - u)

            for c in range(4):
                act.wait_ge(first_gathered, c + 1)
                nc.scalar.copy(first_xg[:, 2 * c:2 * c + 2, :, :],
                               first_bank[c][:].rearrange("p (k u n) -> p k u n", k=2, u=2)).then_inc(first_copied, 1)

            nc.scalar.activation(sig[:, 0, 0:1], eps[:, 0:1], ACT.Silu)
            copy_info(0, 0)
            for p in range(2):
                pair(p, p)
            with act.Fori(1, PAIRS // 2 - 1) as i:
                for u in range(2):
                    pair(i * 2 + u, u)
            for p in range(PAIRS - 2, PAIRS):
                pair(p, p % 2, last=(p == PAIRS - 1))
            load = act.value_load(load_i[0:1, 0:1], min_val=0, max_val=SEQ)
            with act.If(load > WIN):
                with act.Fori(0, EXPERTS) as e:
                    for u in range(2):
                        n = e * 2 + (PAIRS + u)
                        copy_info(n, u)
                        swish(n)
                        copy_hT(n)
                        split_y_hi(n)
            for t in range(TT):
                act.wait_ge(ln_var, TT + t + 1)
                nc.scalar.activation(mv[:, t, 2:3], mv[:, t, 1:2], ACT.Sqrt, bias=eps[:, 0:1]).then_inc(ln_std, 1)

        @block.vector
        def _(dve):
            steps = [0]

            def chained(ins):
                steps[0] += 1
                ins.then_inc(dve_step, 1)
                dve.wait_ge(dve_step, steps[0])

            def split_lo(b):
                n = splits_before(b)
                dve.wait_ge(w_hi_done, n + 1)
                nc.vector.tensor_tensor(w_lo[:, n % SPLIT, :], raw[:, b % RAW, :],
                                        w_hi[:, n % SPLIT, :].bitcast(F32), ALU.subtract).then_inc(w_lo_done, 1)

            def conv_taps():
                n = 0
                for m in range(0, KT, 2):
                    dve.wait_ge(first_tap_done, m + 2)
                    for tap in range(1, CONV_WIDTH):
                        for i in (m, m + 1):
                            if tap > 1:
                                dve.wait_ge(taps_done, n - 1)
                            w = par[:, A_WDW + i * CONV_WIDTH + tap:A_WDW + i * CONV_WIDTH + tap + 1]
                            ins = nc.vector.scalar_tensor_tensor(acc[:, i, :], h_pad[:, i, tap:tap + SEQ], w,
                                                                 acc[:, i, :], ALU.mult, ALU.add)
                            ins.then_inc(taps_done, 1)
                            n += 1
                            yield m

            taps = conv_taps()
            done = [0]

            def some_taps(count, ready):
                for _ in range(count):
                    m = done[0] // (2 * (CONV_WIDTH - 1)) * 2
                    if m + 2 > ready or done[0] >= DVE_TAPS:
                        return
                    next(taps)
                    done[0] += 1

            def evacuate(q):
                src = pair_bank[q % PSUM_PAIRS]
                if q < Q_BLOCK // 2:
                    dve.wait_ge(sigmoid_done, q + 1)
                    nc.vector.tensor_tensor(h_pad[:, q, PAD:PAD + SEQ], src[:, 0:SEQ], sig[:, q % 2, :],
                                            ALU.mult).then_inc(glu_done, 1)
                    dve.wait_ge(glu_done, q + 1)
                elif N_IN // 2 <= q < B_CONV // 2:
                    m = q - N_IN // 2
                    dve.wait_ge(block_done, 2 * q + 2)
                    dve.wait_ge(gates_done, N_IN // 2 - GATE_BLOCK // 2)
                    g = gates[:, KT + 2 * m:KT + 2 * m + 2, :]
                    nc.vector.tensor_tensor(g, src[:].rearrange("p (a t) -> p a t", a=2), g,
                                            ALU.mult).then_inc(attn_gated, 1)
                elif q >= B_CONV // 2:
                    m = q - B_CONV // 2
                    g, other = gates[:, 2 * m:2 * m + 2, :], gates[:, KT + 2 * m:KT + 2 * m + 2, :]
                    dve.wait_ge(block_done, 2 * q + 2)
                    nc.vector.tensor_tensor(g, src[:].rearrange("p (a t) -> p a t", a=2), g,
                                            ALU.mult).then_inc(conv_gated, 1)
                    dve.wait_ge(conv_gated, m + 1)
                    dve.wait_ge(attn_gated, m + 1)
                    nc.vector.tensor_tensor(g, g, other, ALU.add).then_inc(merged, 1)
                    dve.wait_ge(m_hi_done, m + 1)
                    nc.vector.tensor_tensor(a_lo[:, 2 * m:2 * m + 2, :], g,
                                            a_hi[:, 2 * m:2 * m + 2, :].bitcast(F32),
                                            ALU.subtract).then_inc(m_lo_done, 1)

            def take_scores(h):
                dve.wait_ge(scores_done, h + 1)
                slope = 2.0 ** (-8.0 * (h + 1) / HEADS)
                nc.vector.scalar_tensor_tensor(prob[:, h, :, :].rearrange("p t n -> p (t n)"), dist, -slope / SCALE,
                                               score_bank[h % 2][:], ALU.mult, ALU.add).then_inc(scores_read, 1)
                if h % 2:
                    dve.wait_ge(scores_read, h + 1)
                    n = TT * (h - 1)
                    chained(nc.vector.tensor_reduce(small[:, 0, n:n + 4],
                                                    prob[:, h - 1:h + 1, :, :].rearrange("p h t n -> p (h t) n"),
                                                    X_AXIS, ALU.max))
                    nc.vector.scalar_tensor_tensor(
                        small[:, 1, n:n + 4].rearrange("p (h t) -> p h t", h=2),
                        small[:, 0, n:n + 4].rearrange("p (h t) -> p h t", h=2), -SCALE,
                        small[:, 5, h - 1:h + 1].unsqueeze(2).broadcast_to([P, 2, TT]),
                        ALU.mult, ALU.min).then_inc(neg_max_done, 1)

            def sinks():
                dve.wait_ge(neg_max_done, HEADS // 2)
                nc.vector.tensor_tensor(small[:, 3, :].rearrange("p (h t) -> p h t", h=HEADS),
                                        small[:, 1, :].rearrange("p (h t) -> p h t", h=HEADS),
                                        row[:, R_SINK:R_SINK + HEADS].unsqueeze(2).broadcast_to([P, HEADS, TT]),
                                        ALU.add).then_inc(sink_in, 1)

            def denominators():
                dve.wait_ge(exp_done, HEADS)
                dve.wait_ge(sink_exp, 1)
                chained(nc.vector.tensor_tensor(small[:, 6, :], small[:, 2, :], small[:, 4, :], ALU.add))
                nc.vector.reciprocal(small[:, 7, :], small[:, 6, :]).then_inc(denominators_done, 1)

            def split_o(h):
                dve.wait_ge(o_hi_done, h + 1)
                nc.vector.tensor_tensor(a_lo[:, h, :], o_bank[h % 2][:, 0:SEQ], a_hi[:, h, :].bitcast(F32),
                                        ALU.subtract).then_inc(o_lo_done, 1)

            def layer_norm(n, lnr, s_rows, psum, ready):
                def statistics(t, c):
                    ins = nc.vector.bn_stats(stat[:, t, c, :], psum[2 * t + c][:])
                    if c:
                        chained(ins)
                        nc.vector.bn_aggr(mv[:, t, 0:2], stat[:, t, :, :]).then_inc(ln_var, 1)

                def normal(t, c):
                    v, m = xt[:, t, c * HALF:(c + 1) * HALF], slice(c * HALF, (c + 1) * HALF)
                    chained(nc.vector.scalar_tensor_tensor(v, psum[2 * t + c][:], mv[:, t, 0:1], lnr[:, 0, m],
                                                           ALU.subtract, ALU.mult))
                    nc.vector.scalar_tensor_tensor(v, v, mv[:, t, 3:4], lnr[:, 1, m], ALU.mult,
                                                   ALU.add).then_inc(ready, 1)

                def deviation(t):
                    dve.wait_ge(ln_std, TT * n + t + 1)
                    chained(nc.vector.reciprocal(mv[:, t, 3:4], mv[:, t, 2:3]))

                statistics(0, 0)
                statistics(0, 1)
                statistics(1, 0)
                dve.wait_ge(s_rows, 16)
                deviation(0)
                normal(0, 0)
                statistics(1, 1)
                normal(0, 1)
                deviation(1)
                normal(1, 0)
                normal(1, 1)

            for c in range(2):
                k = slice(4 * c, 4 * c + 4)
                dve.wait_ge(x_hi_done, c + 1)
                nc.vector.tensor_tensor(x_lo[:, k, :], xT_raw[:, k, :], x_hi[:, k, :].bitcast(F32),
                                        ALU.subtract).then_inc(x_lo_done, 1)
            for b in range(N_BLOCKS):
                if b == B_CONV:
                    some_taps(DVE_TAPS, KT)
                    dve.wait_ge(mean_done, 1)
                    for m in range(0, KT, 2):
                        nc.vector.tensor_tensor(acc[:, m:m + 2, :], acc[:, m:m + 2, :],
                                                bank[7][:, 0:SEQ].unsqueeze(1).broadcast_to([P, 2, SEQ]),
                                                ALU.subtract).then_inc(centered, 1)
                    split_lo(b)
                    split_lo(b + 1)
                    dve.wait_ge(std_done, 1)
                    chained(nc.vector.reciprocal(sig[:, 1, :], sig[:, 0, :]))
                    dve.wait_ge(squared, KT // 2)
                    for i in range(KT):
                        nc.vector.tensor_tensor(acc[:, i, :], acc[:, i, :], sig[:, 1, :],
                                                ALU.mult).then_inc(scaled, 1)
                    for i in range(KT):
                        dve.wait_ge(c_hi_done, i + 1)
                        nc.vector.tensor_tensor(x_lo[:, i, :], acc[:, i, :], x_hi[:, i, :].bitcast(F32),
                                                ALU.subtract).then_inc(c_lo_done, 1)
                if b not in NATIVE and b not in (B_CONV, B_CONV + 1):
                    split_lo(b)
                if b == 2:
                    dve.wait_ge(consts_set, 4)
                    dve.wait_ge(s_par, 16)
                    dve.wait_ge(s_con, 16)
                    dve.wait_ge(s_row, 16)
                    dve.wait_ge(s_dist, 16)
                    chained(nc.vector.tensor_scalar(small[:, 5, 0:HEADS], row[:, R_SINK:R_SINK + HEADS], -1.0, None,
                                                    ALU.mult))
                if b % 2 and b >= 3 and (b - 3) // 2 < B_OUT // 2:
                    evacuate((b - 3) // 2)
                if 30 <= b <= 33:
                    take_scores(2 * (b - 30))
                    take_scores(2 * (b - 30) + 1)
                    if b == 33:
                        sinks()
                if b == 35:
                    denominators()
                if 39 <= b < 39 + HEADS:
                    split_o(b - 39)
                if b < B_CONV:
                    some_taps(TAPS_PER_BLOCK, (b - 5) // 2 + 1 if b >= 5 else 0)
            dve.wait_ge(block_done, N_BLOCKS)
            layer_norm(0, ln_rows, s_ln1, out_bank, x1_ready)
            for t in range(TT):
                dve.wait_ge(x1_hi_done, t + 1)
                nc.vector.tensor_tensor(x1_lo[:, t, :], xt[:, t, :], x1_hi[:, t, :].bitcast(F32),
                                        ALU.subtract).then_inc(x1_lo_done, 1)

            def per_token(col, n):
                return col.unsqueeze(2).broadcast_to([P, TT, n])

            dve.wait_ge(logits_done, 1)
            chained(nc.vector.tensor_tensor(lg[:], bank[3][:, 0:TT * LOGITS].rearrange("p (t n) -> p t n", t=TT),
                                            row[:, R_BIAS:R_BIAS + LOGITS].unsqueeze(1).broadcast_to([P, TT, LOGITS]),
                                            ALU.add))
            g_log = lg[:, :, 0:GROUPS]
            chained(nc.vector.tensor_reduce(rs[:, 0, :], g_log, X_AXIS, ALU.max))
            nc.vector.tensor_tensor(rg[:, 1, :, :], g_log, per_token(rs[:, 0, :], GROUPS),
                                    ALU.subtract).then_inc(exp_in, 1)
            chained(nc.vector.tensor_tensor(rg[:, 0, :, :], g_log, per_token(rs[:, 0, :], GROUPS), ALU.is_equal))
            chained(nc.vector.tensor_tensor(rg[:, 0, :, :], rg[:, 0, :, :],
                                            rank4.unsqueeze(1).broadcast_to([P, TT, GROUPS]), ALU.mult))
            chained(nc.vector.tensor_reduce(rs[:, 1, :], rg[:, 0, :, :], X_AXIS, ALU.max))
            chained(nc.vector.tensor_tensor(rg[:, 3, :, :], rg[:, 0, :, :], per_token(rs[:, 1, :], GROUPS),
                                            ALU.is_equal))
            nc.vector.tensor_scalar(rg[:, 0, :, :], rg[:, 3, :, :], NEVER, -NEVER, ALU.mult, ALU.add)
            e_log = lg[:, :, GROUPS:].rearrange("p t (g e) -> p t g e", g=GROUPS)

            def by_group(a):
                return a.unsqueeze(3).broadcast_to([P, TT, GROUPS, PER_GROUP])

            def grouped(a):
                return a.rearrange("p t (g e) -> p t g e", g=GROUPS)

            chained(nc.vector.tensor_tensor(grouped(rt[:, 0, :, :]), e_log, by_group(rg[:, 3, :, :]), ALU.mult))
            chained(nc.vector.tensor_tensor(grouped(rt[:, 1, :, :]), grouped(rt[:, 0, :, :]),
                                            by_group(rg[:, 0, :, :]), ALU.add))

            def first_of_largest(logit, one_hot, largest, key):
                chained(nc.vector.tensor_reduce(largest, logit, X_AXIS, ALU.max))
                chained(nc.vector.tensor_tensor(rt[:, 7, :, :], logit, per_token(largest, EXPERTS), ALU.is_equal))
                chained(nc.vector.tensor_tensor(rt[:, 7, :, :], rt[:, 7, :, :],
                                                rank32.unsqueeze(1).broadcast_to([P, TT, EXPERTS]), ALU.mult))
                chained(nc.vector.tensor_reduce(key, rt[:, 7, :, :], X_AXIS, ALU.max))
                chained(nc.vector.tensor_tensor(one_hot, rt[:, 7, :, :], per_token(key, EXPERTS), ALU.is_equal))

            first_of_largest(rt[:, 1, :, :], rt[:, 2, :, :], rs[:, 2, :], rs[:, 3, :])
            chained(nc.vector.scalar_tensor_tensor(rt[:, 3, :, :], rt[:, 2, :, :], -2 * NEVER, rt[:, 1, :, :],
                                                   ALU.mult, ALU.add))
            first_of_largest(rt[:, 3, :, :], rt[:, 4, :, :], rs[:, 4, :], rs[:, 5, :])
            nc.vector.tensor_tensor(rs[:, 7, :], rs[:, 4, :], rs[:, 2, :], ALU.subtract).then_inc(exp_in, 1)
            nc.vector.tensor_tensor(rt[:, 5, :, :], rt[:, 2, :, :], rt[:, 4, :, :], ALU.add).then_inc(onehot_done, 1)
            nc.vector.tensor_copy(rt[:, 8, :, :], rt[:, 2, :, :])
            dve.wait_ge(onehot_done, 1)
            dve.wait_ge(ranks_done, 1)
            rank = bank[4][:, 0:TT * EXPERTS].rearrange("p (t n) -> p t n", t=TT)
            place = rt[:, 0, :, :]
            chained(nc.vector.scalar_tensor_tensor(place, rank, 1.0, rt[:, 5, :, :], ALU.add, ALU.mult))
            nc.vector.tensor_tensor(
                first_places.rearrange("p t (j s) -> p t j s", j=4),
                iota[:, 0:WIN].unsqueeze(1).unsqueeze(1).broadcast_to([P, TT, 4, WIN]),
                place[:, :, 0:4].unsqueeze(3).broadcast_to([P, TT, 4, WIN]), ALU.is_equal).then_inc(first_built, 1)
            dve.wait_ge(router_exp, 2)
            chained(nc.vector.tensor_reduce(rs[:, 6, :], rg[:, 2, :, :], X_AXIS, ALU.add))
            chained(nc.vector.tensor_scalar(rs[:, 9, :], rs[:, 8, :], 1.0, None, ALU.add))
            chained(nc.vector.tensor_tensor(rs[:, 10, :], rs[:, 9, :], rs[:, 6, :], ALU.mult))
            chained(nc.vector.reciprocal(rs[:, 11, :], rs[:, 10, :]))
            chained(nc.vector.tensor_tensor(rs[:, 12, :], rs[:, 11, :], rs[:, 8, :], ALU.mult))
            nc.vector.tensor_tensor(rt[:, 2, :, :], rt[:, 2, :, :], per_token(rs[:, 11, :], EXPERTS), ALU.mult)
            chained(nc.vector.tensor_tensor(rt[:, 7, :, :], rt[:, 4, :, :], per_token(rs[:, 12, :], EXPERTS),
                                            ALU.mult))
            chained(nc.vector.tensor_tensor(rt[:, 6, :, :], rt[:, 2, :, :], rt[:, 7, :, :], ALU.add))
            chained(nc.vector.tensor_copy(rt[:, 9, 0, :], bank[5][:, 0:EXPERTS]))
            chained(nc.vector.tensor_tensor_scan(rt[:, 9, 1, :], ones[:, 0:EXPERTS], rt[:, 9, 0, :], 0.0,
                                                 ALU.mult, ALU.add))
            chained(nc.vector.tensor_tensor(rt[:, 9, 1, :], rt[:, 9, 1, :], rt[:, 9, 0, :], ALU.subtract))
            chained(nc.vector.scalar_tensor_tensor(rt[:, 3, :, :], rank, 1.0,
                                                   rt[:, 9, 1, :].unsqueeze(1).broadcast_to([P, TT, EXPERTS]),
                                                   ALU.add, ALU.add))
            for n, one_hot in enumerate((rt[:, 8, :, :], rt[:, 4, :, :])):
                chained(nc.vector.tensor_tensor(rt[:, 1, :, :], rt[:, 3, :, :], one_hot, ALU.mult))
                chained(nc.vector.tensor_reduce(rs[:, 13 + n, :], rt[:, 1, :, :], X_AXIS, ALU.add))
            for t in range(TT):
                nc.vector.tensor_scalar(first_choice[:, t, :], iota, rs[:, 13, t:t + 1], None, ALU.is_equal)
            for t in range(TT):
                if t == 0:
                    chained(nc.vector.tensor_reduce(load_f[:], rt[0:1, 9, 0, :], X_AXIS, ALU.max))
                nc.vector.scalar_tensor_tensor(compact[:, t, :], iota, rs[:, 14, t:t + 1], first_choice[:, t, :],
                                               ALU.is_equal, ALU.add).then_inc(compact_built, 1)
            for w in range(WINDOWS + 1):
                nc.vector.tensor_scalar(starts_f[:, w, :], rt[0:1, 9, 1, :], float(WIN * w), float(ROUTED),
                                        ALU.add, ALU.min)
            nc.vector.tensor_copy(load_i[:], load_f[:])
            for u in range(2):
                ins = nc.vector.tensor_copy(info[u][:, :, 0:1], con[:, C_TOKEN:C_TOKEN + TT].unsqueeze(2))
            chained(ins)
            nc.vector.tensor_copy(starts[:], starts_f).then_inc(load_known, 1)

            def build_gather(p, u):
                if from_pair(p, 2):
                    dve.wait_ge(info_done, p - 1)
                two = bass.ds(p * 2, 2)
                nc.vector.tensor_tensor(
                    gat[u].rearrange("p t (j s) -> p t j s", j=2),
                    iota[:, 0:WIN].unsqueeze(1).unsqueeze(1).broadcast_to([P, TT, 2, WIN]),
                    place[:, :, two].unsqueeze(3).broadcast_to([P, TT, 2, WIN]), ALU.is_equal)
                nc.vector.tensor_copy(info[u][:, :, 1:3], rt[:, 6, :, two]).then_inc(gat_built, 1)

            def build_more(e, n, u):
                dve.wait_ge(info_done, n - 1)
                nc.vector.memset(sig[:, 0, 0:1], 0.0)
                for j in range(2):
                    nc.vector.tensor_copy(info[u][:, :, 1 + j:2 + j], rt[:, 6, :, bass.ds(e, 1)])
                    ins = nc.vector.tensor_copy(more_place[:, :, j:j + 1], place[:, :, bass.ds(e, 1)])
                ins.then_inc(more_copied, 1)
                dve.wait_ge(more_copied, e * 2 + (u + 1))
                for j in range(2):
                    ins = nc.vector.scalar_tensor_tensor(
                        gat[u][:, :, j * WIN:(j + 1) * WIN],
                        iota[:, 0:WIN].unsqueeze(1).broadcast_to([P, TT, WIN]), float(WIN * (1 + 2 * u + j)),
                        more_place[:, :, j:j + 1].broadcast_to([P, TT, WIN]), ALU.add, ALU.is_equal)
                ins.then_inc(gat_built, 1)

            def gate_times_up(p, u):
                dve.wait_ge(swish_done, p + 1)
                dve.wait_ge(info_copied, p + 1)
                if from_pair(p, 1):
                    dve.wait_ge(h_turned, p)
                nc.vector.scalar_tensor_tensor(h_sb, swished, weight[u], gu_bank[:, HIDDEN:], ALU.mult,
                                               ALU.mult).then_inc(h_ready, 1)

            def build_scatter(p, u):
                if from_pair(p, 2):
                    dve.wait_ge(scattered, p - 1)
                nc.vector.tensor_scalar(scatter_matrix[u], iota[:, 0:SEQ], token[u], None,
                                        ALU.is_equal).then_inc(scatter_built, 1)

            def split_y_lo(p):
                for c in range(2):
                    n = slice(c * HALF, (c + 1) * HALF)
                    dve.wait_ge(y_hi_done, 2 * p + (c + 1))
                    nc.vector.tensor_tensor(y_lo[:, n], y_bank[c][:], y_hi[:, n].bitcast(F32),
                                            ALU.subtract).then_inc(y_lo_done, 1)

            def copy_sorted():
                for k in range(1, KT, 2):
                    dve.wait_ge(gathered, k + 1)
                    nc.vector.tensor_copy(xgT[:, k, 0:ROUTED], out_bank[k % 4][:]).then_inc(xgT_odd, 1)

            def pair(p, u, build=True):
                gate_times_up(p, u)
                if is_pair(p, 1):
                    copy_sorted()
                build_scatter(p, u)
                if build:
                    build_gather(p + 2, u)
                split_y_lo(p)

            build_gather(0, 0)
            build_gather(1, 1)
            for p in range(2):
                pair(p, p)
            with dve.Fori(1, PAIRS // 2 - 1) as i:
                for u in range(2):
                    pair(i * 2 + u, u)
            for p in range(PAIRS - 2, PAIRS):
                pair(p, p % 2, build=False)
            load = dve.value_load(load_i[0:1, 0:1], min_val=0, max_val=SEQ)
            with dve.If(load > WIN):
                with dve.Fori(0, EXPERTS) as e:
                    for u in range(2):
                        n = e * 2 + (PAIRS + u)
                        build_more(e, n, u)
                        gate_times_up(n, u)
                        build_scatter(n, u)
                        split_y_lo(n)
                dve.wait_ge(scattered, PAIRS + 2 * EXPERTS)

            dve.wait_ge(scattered, PAIRS)
            layer_norm(1, ln2_rows, s_ln2, out_bank, result)

        @block.tensor
        def _(pe):
            mm = nc.tensor.matmul

            def three_products(dst, pairs, first, last, **kw):
                (ah, al), (bh, bl) = pairs
                mm(dst, ah, bh, start=first, stop=False, **kw)
                mm(dst, ah, bl, start=False, stop=False, **kw)
                return mm(dst, al, bh, start=False, stop=last, **kw)

            def column_block(b, hi, lo, tile_ready=None):
                q = b // 2
                dst = pair_bank[q % PSUM_PAIRS][:, (b % 2) * SEQ:(b % 2 + 1) * SEQ]
                if b % 2 == 0 and q >= PSUM_PAIRS:
                    wait_pair_read(pe, q - PSUM_PAIRS)
                n = splits_before(b)
                if b in NATIVE:
                    pe.wait_ge(raw_loaded[b % RAW], 16 * (b // RAW + 1))
                else:
                    pe.wait_ge(w_lo_done, n + 1)
                for k in range(KT):
                    if tile_ready is not None:
                        pe.wait_ge(tile_ready, k + 1)
                    w = slice(k * P, (k + 1) * P)
                    if b in NATIVE:
                        if b == 0 and k % 4 == 0:
                            pe.wait_ge(s_xT[k // 4], 16)
                        ins = mm(dst, raw[:, b % RAW, w], xT_raw[:, k, :], start=(k == 0), stop=(k == KT - 1))
                    else:
                        ins = three_products(dst, ((w_hi[:, n % SPLIT, w], w_lo[:, n % SPLIT, w]),
                                                   (hi[:, k, :], lo[:, k, :])), k == 0, k == KT - 1)
                ins.then_inc(block_done, 1)

            def scores(h):
                if h == 0:
                    pe.wait_ge(qkv_copied, (V_BLOCK - Q_BLOCK) // 2)
                if h >= 2:
                    pe.wait_ge(scores_read, h - 1)
                for t in range(TT):
                    ins = mm(score_bank[h % 2][:, t * SEQ:(t + 1) * SEQ], qT[:, h, t * P:(t + 1) * P],
                             kT[:, h // 2, :], start=True, stop=True)
                ins.then_inc(scores_done, 1)

            def turn_v():
                pe.wait_ge(qkv_copied, (GATE_BLOCK - Q_BLOCK) // 2)
                for t in range(TT):
                    for j in range(KV_HEADS):
                        ins = nc.tensor.transpose(o_bank[t][:, j * P:(j + 1) * P], vT[:, j, t * P:(t + 1) * P], ident)
                ins.then_inc(v_turned, 1)

            def turn_p(h):
                pe.wait_ge(prob_ready, h + 1)
                if h >= 1:
                    pe.wait_ge(p_copied, h)
                for kb in range(TT):
                    for t in range(TT):
                        ins = nc.tensor.transpose(t_bank[:, kb * SEQ + t * P:kb * SEQ + (t + 1) * P],
                                                  prob[:, h, t, kb * P:(kb + 1) * P], ident)
                ins.then_inc(p_turned, 1)

            def values(h):
                pe.wait_ge(p_copied, h + 1)
                if h == 0:
                    pe.wait_ge(v_copied, 1)
                if h >= 2:
                    pe.wait_ge(o_lo_done, h - 1)
                for kb in range(TT):
                    ins = mm(o_bank[h % 2][:, 0:SEQ], v_sb[:, kb, (h // 2) * P:(h // 2 + 1) * P],
                             pT[:, h % 2, kb, :], start=(kb == 0), stop=(kb == TT - 1))
                ins.then_inc(pv_done, 1)

            def residual(first):
                for t in range(TT):
                    for c in range(2):
                        mm(out_bank[2 * t + c][:], alpha_ident[:], xt[:, t, c * HALF:(c + 1) * HALF],
                                 start=first, stop=True, skip_group_check=True)

            for b in range(N_IN):
                if b == 2:
                    pe.wait_ge(x_lo_done, 2)
                if b == 24:
                    pe.wait_ge(s_con, 16)
                column_block(b, x_hi, x_lo)
                if 29 <= b <= 32:
                    scores(2 * (b - 29))
                    scores(2 * (b - 29) + 1)
                if b == 34:
                    turn_v()
                if 36 <= b < 36 + HEADS:
                    turn_p(b - 36)
                if 37 <= b < 37 + HEADS:
                    values(b - 37)
            def mean(i):
                return mm(bank[7][:, 0:SEQ], mean_ones[:], acc[:, i, :], start=(i == 0), stop=(i == KT - 1))

            for b in range(B_ATTN, B_CONV - 2):
                column_block(b, a_hi, a_lo, o_lo_done if b == B_ATTN else None)
                if b == B_CONV - 4:
                    pe.wait_ge(taps_done, DVE_TAPS // KT * (KT - 2))
                    for i in range(KT - 2):
                        mean(i)
            pe.wait_ge(taps_done, DVE_TAPS)
            for i in range(KT - 2, KT):
                ins = mean(i)
            ins.then_inc(mean_done, 1)
            for b in range(B_CONV - 2, B_CONV):
                column_block(b, a_hi, a_lo)
            wait_pair_read(pe, VAR_PAIR - PSUM_PAIRS)
            for i in range(KT):
                if i % 2 == 0:
                    pe.wait_ge(squared, i // 2 + 1)
                ins = mm(var_bank[:, 0:SEQ], mean_ones[:], square[:, i, :], start=(i == 0), stop=(i == KT - 1))
            ins.then_inc(var_done, 1)
            pe.wait_ge(s_xt, 16)
            pe.wait_ge(alpha_set, 1)
            residual(first=True)
            for b in range(B_CONV, B_OUT):
                column_block(b, x_hi, x_lo, c_lo_done if b == B_CONV else None)
            for b in range(B_OUT, N_BLOCKS):
                k = b - B_OUT
                s = splits_before(b)
                pe.wait_ge(w_lo_done, s + 1)
                pe.wait_ge(m_lo_done, k // 2 + 1)
                for t in range(TT):
                    for c in range(2):
                        n = slice(c * HALF, (c + 1) * HALF)
                        m = slice(t * P, (t + 1) * P)
                        ins = three_products(out_bank[2 * t + c][:], ((a_hi[:, k, m], a_lo[:, k, m]),
                                             (w_hi[:, s % SPLIT, n], w_lo[:, s % SPLIT, n])), False, k == KT - 1,
                                             skip_group_check=True)
                ins.then_inc(block_done, 1)

            for t in range(TT):
                for c in range(2):
                    pe.wait_ge(x1_ready, 2 * t + c + 1)
                    dst = (pair_bank + [bank[7]])[2 * t + c]
                    for i in range(4):
                        ins = nc.tensor.transpose(dst[:, i * P:(i + 1) * P],
                                                  xt[:, t, (4 * c + i) * P:(4 * c + i + 1) * P], ident)
                    ins.then_inc(x1_turned, 1)
                pe.wait_ge(s_wr, 16)
                pe.wait_ge(x1T_copied, 2 * t + 2)
                for k in range(KT):
                    ins = mm(bank[3][:, t * LOGITS:(t + 1) * LOGITS], x1T[:, k, t * P:(t + 1) * P], wr[:, k, :],
                             start=(k == 0), stop=(k == KT - 1))
            ins.then_inc(logits_done, 1)
            one_hot = rt[:, 5, :, :]
            pe.wait_ge(onehot_done, 1)
            mm(bank[4][:, 0:EXPERTS], tri, one_hot[:, 0, :], start=True, stop=True)
            mm(bank[4][:, EXPERTS:2 * EXPERTS], ones[:], one_hot[:, 0, :], start=True, stop=False)
            mm(bank[4][:, EXPERTS:2 * EXPERTS], tri, one_hot[:, 1, :], start=False, stop=True)
            mm(bank[5][:, 0:EXPERTS], ones[:], one_hot[:, 0, :], start=True, stop=False)
            mm(bank[5][:, 0:EXPERTS], ones[:], one_hot[:, 1, :], start=False, stop=True).then_inc(ranks_done, 1)

            def gather_first():
                pe.wait_ge(x1_lo_done, TT)
                pe.wait_ge(first_built, 1)
                for k in range(KT):
                    n = slice(k * P, (k + 1) * P)
                    dst = first_bank[k // 2][:, (k % 2) * SEQ:(k % 2 + 1) * SEQ]
                    for t in range(TT):
                        mm(dst, x1_hi[:, t, n], first_places[:, t, :], start=(t == 0), stop=False)
                        ins = mm(dst, x1_lo[:, t, n], first_places[:, t, :], start=False, stop=(t == TT - 1))
                    if k % 2:
                        ins.then_inc(first_gathered, 1)

            def gather_sorted():
                pe.wait_ge(compact_built, TT)
                for k in range(KT):
                    if k >= 4:
                        pe.wait_ge(xgT_odd if k % 2 else xgT_even, (k - 4) // 2 + 1)
                    n = slice(k * P, (k + 1) * P)
                    for t in range(TT):
                        mm(out_bank[k % 4][:], x1_hi[:, t, n], compact[:, t, :], start=(t == 0), stop=False)
                        ins = mm(out_bank[k % 4][:], x1_lo[:, t, n], compact[:, t, :], start=False,
                                 stop=(t == TT - 1))
                    ins.then_inc(gathered, 1)

            def slot_info(p, u):
                pe.wait_ge(gat_built, p + 1)
                if from_pair(p, 1):
                    pe.wait_ge(hT_copied, p)
                for t in range(TT):
                    ins = mm(turn_bank[:, 0:3], gat[u][:, t, :], info[u][:, t, :], start=(t == 0), stop=(t == TT - 1))
                ins.then_inc(info_done, 1)

            def gate_up(p, u, turn, more=False):
                if from_pair(p, 2):
                    pe.wait_ge(xg_ready, p - 1)
                if from_pair(p, 1):
                    pe.wait_ge(h_ready, p)
                for k in range(KT):
                    c = k // (KT // 2)
                    if is_pair(p, 0) and k % 2 == 0:
                        pe.wait_ge(first_copied, k // 2 + 1)
                    for j in range(2):
                        s = 0 if more else 2 * u + j
                        w = slots[:, s, k * 2 * HIDDEN:(k + 1) * 2 * HIDDEN]
                        if not more and is_pair(p, 2) and j == 0:
                            w = spare[c][:, k % (KT // 2) * 2 * HIDDEN:(k % (KT // 2) + 1) * 2 * HIDDEN]
                            if k % (KT // 2) == 0:
                                pe.wait_ge(spare_loaded[c], 16)
                        elif not more and k % (KT // 2) == 0:
                            n = turn - 1 if s == 0 and from_pair(p, 4) else turn
                            pe.wait_ge(gu_loaded[s][c], 16 * n)
                        ins = mm(gu_bank[j * WIN:(j + 1) * WIN, :], xg[u][:, k, j * WIN:(j + 1) * WIN], w,
                                 start=(k == 0), stop=(k == KT - 1))
                ins.then_inc(gu_done, 1)

            def turn_h(p):
                pe.wait_ge(h_ready, p + 1)
                pe.wait_ge(info_copied, p + 1)
                for k in range(HT):
                    ins = nc.tensor.transpose(turn_bank[:, k * P:(k + 1) * P], h_sb[:, k * P:(k + 1) * P], ident)
                ins.then_inc(h_turned, 1)

            def down(p, slot):
                pe.wait_ge(hT_copied, p + 1)
                if from_pair(p, 1):
                    pe.wait_ge(y_lo_done, 2 * p)
                for c in range(2):
                    for k in range(HT):
                        for j in range(2):
                            w = slots[:, slot[j], GU_N:SLOT_N].rearrange("p (k n) -> p k n", k=HT)
                            ins = mm(y_bank[c][j * WIN:(j + 1) * WIN, :], hT[:, k, j * WIN:(j + 1) * WIN],
                                     w[:, k, c * HALF:(c + 1) * HALF], start=(k == 0), stop=(k == HT - 1))
                    ins.then_inc(down_done, 1)

            def scatter(p, u, first=False):
                pe.wait_ge(scatter_built, p + 1)
                for c in range(2):
                    pe.wait_ge(y_lo_done, 2 * p + (c + 1))
                    for t in range(TT):
                        dst = out_bank[2 * t + c][:]
                        s = scatter_matrix[u][:, t * P:(t + 1) * P]
                        n = slice(c * HALF, (c + 1) * HALF)
                        mm(dst, s, y_hi[:, n], start=first, stop=False, skip_group_check=True)
                        ins = mm(dst, s, y_lo[:, n], start=False, stop=True, skip_group_check=True)
                ins.then_inc(scattered, 1)

            def pair(p, u, turn, last=False):
                if last:
                    residual(first=False)
                    scatter(p - 1, 1 - u)
                if from_pair(p, 1):
                    gate_up(p, u, turn)
                    if is_pair(p, 1):
                        gather_sorted()
                        pe.wait_ge(xgT_odd, KT // 2)
                        pe.wait_ge(xgT_even, KT // 2)
                    if not last:
                        scatter(p - 1, 1 - u, first=is_pair(p, 1))
                turn_h(p)
                for j in range(2):
                    pe.wait_ge(wd_loaded[2 * u + j], 16 * turn)
                down(p, (2 * u, 2 * u + 1))
                if not last:
                    slot_info(p + 1, 1 - u)

            gather_first()
            gate_up(0, 0, 1)
            slot_info(0, 0)
            for p in range(4):
                pair(p, p % 2, p // 2 + 1)
            with pe.Fori(2, PAIRS // 2 - 1) as i:
                for u in range(2):
                    pair(i * 2 + u, u, i + 1)
            for p in range(PAIRS - 2, PAIRS):
                pair(p, p % 2, PAIRS // 2, last=(p == PAIRS - 1))
            scatter(PAIRS - 1, 1)

            load = pe.value_load(load_i[0:1, 0:1], min_val=0, max_val=SEQ)
            with pe.If(load > WIN):
                with pe.Fori(0, EXPERTS) as e:
                    pe.wait_ge(more_loaded, e * 32 + 32)
                    for u in range(2):
                        n = e * 2 + (PAIRS + u)
                        slot_info(n, u)
                        gate_up(n, u, 0, more=True)
                        turn_h(n)
                        down(n, (0, 0))
                        scatter(n, u)


def kernel(x, w_in, b_gate, w_dw, b_dw, conv_ln_g, conv_ln_b, w_conv_proj, attn_sink, w_attn_proj, w_out,
           ln1_g, ln1_b, w_router_group, b_router_group, w_router_expert, b_router_expert, w_gate_up, w_down,
           ln2_g, ln2_b):
    import concourse.bacc as bacc
    from concourse.bass_utils import run_bass_kernel_spmd

    def blocks(w, n):
        return w.reshape(KT, P, n, P).transpose(2, 1, 0, 3).reshape(n, P, KT * P)

    def channels(v):
        return v.reshape(KT, P, -1).transpose(1, 0, 2).reshape(P, -1)

    given = {k: np.asarray(v) for k, v in dict(
        x=x, w_in=w_in, b_gate=b_gate, w_dw=w_dw, b_dw=b_dw, g=conv_ln_g, b=conv_ln_b, w_conv=w_conv_proj,
        sink=attn_sink, w_attn=w_attn_proj, w_out=w_out, ln1_g=ln1_g, ln1_b=ln1_b, rg=w_router_group,
        brg=b_router_group, re=w_router_expert, bre=b_router_expert, gu=w_gate_up, wd=w_down, ln2_g=ln2_g,
        ln2_b=ln2_b).items()}
    g = {k: v[0] for k, v in given.items()}
    arrays = {
        "xT": g["x"].T.reshape(KT, P, SEQ).transpose(1, 0, 2),
        "x": g["x"],
        "consts": constants(),
        "dists": distances(),
        "chan": np.concatenate([g["b_gate"].reshape(2 * KT, P).T, channels(g["w_dw"].T), channels(g["b_dw"]),
                                channels(g["g"]), channels(g["b"])], axis=1),
        "rows": np.concatenate([g["brg"], g["bre"], g["sink"]])[None, :],
        "w_in": blocks(g["w_in"], N_IN),
        "w_attn": blocks(g["w_attn"], KT),
        "w_conv": blocks(g["w_conv"], KT),
        "w_out": g["w_out"],
        "ln1": np.stack([g["ln1_g"], g["ln1_b"]])[None],
        "ln2": np.stack([g["ln2_g"], g["ln2_b"]])[None],
        "w_router": np.concatenate([g["rg"], g["re"]], axis=1).reshape(KT, P, LOGITS).transpose(1, 0, 2),
        "w_gate_up": g["gu"].reshape(EXPERTS, KT, P, 2 * HIDDEN).transpose(0, 2, 1, 3).reshape(EXPERTS, P, GU_N),
        "w_down": g["wd"].reshape(EXPERTS, HT, P, D).transpose(0, 2, 1, 3).reshape(EXPERTS, P, WD_N),
    }
    nc = bacc.Bacc("TRN2", target_bir_lowering=False, num_devices=1)
    sent, args = {}, []
    for name, a in arrays.items():
        sent[f"in_{name}"] = np.ascontiguousarray(a)
        args.append(nc.dram_tensor(f"in_{name}", a.shape, F32, kind="ExternalInput").ap())
    out = nc.dram_tensor("out_x", (SEQ, D), F32, kind="ExternalOutput").ap()
    encoder_kernel(nc, *args, out)
    result = run_bass_kernel_spmd(nc, [sent], core_ids=[0])
    return result.results[0]["out_x"].reshape(1, SEQ, D)
```
